# Optimizing a Trainium2 kernel written in Bass

```python
import math
import jax, jax.numpy as jnp
from jax import lax
import numpy as np

D_MODEL = 2048
BATCH = 1
SEQ = 512
DEPTH = 1

CHUNK = 64
ATTN_WINDOW = 128
WINDOW_CHUNKS = ATTN_WINDOW // CHUNK
HEAD_DIM = 64
N_Q_HEADS = D_MODEL // (2 * HEAD_DIM)
N_KV_HEADS = 2
Q_PER_KV = N_Q_HEADS // N_KV_HEADS
ATTN_WIDTH = N_Q_HEADS * HEAD_DIM
KV_WIDTH = N_KV_HEADS * HEAD_DIM
POOL_WINDOWS = (2, 4, 8, 16)
POOL_WIDTH = D_MODEL // 2
N_POOL_GROUPS = len(POOL_WINDOWS)
POOL_GROUP = POOL_WIDTH // N_POOL_GROUPS
IN_WIDTH = ATTN_WIDTH + 2 * KV_WIDTH + POOL_WIDTH + 2 * D_MODEL
PEER_HEADS = 8
N_KEYS = 128
N_EXPERTS = N_KEYS * N_KEYS
PEER_QUERY_DIM = 256
PEER_HALF = PEER_QUERY_DIM // 2
PEER_TOPK = 16
PEER_TOKEN_BLOCK = 128
N_MOD = 6
RMS_EPS = 1e-6

kernel_name = "chunk_causal_hybrid_swa_pool_peer_block"

def rms_norm(x, g):
    xf = x.astype(jnp.float32)
    y = xf * lax.rsqrt(jnp.mean(xf * xf, axis=-1, keepdims=True) + RMS_EPS)
    return (y * g.astype(jnp.float32)).astype(x.dtype)

def modulate(h, shift, scale):
    return h * (1.0 + scale[:, None, :]) + shift[:, None, :]

def chunk_window_attention(q, k, v, sinks):
    B, S = q.shape[0], q.shape[1]
    n_chunks = S // CHUNK
    q = q.reshape(B, n_chunks, CHUNK, N_KV_HEADS, Q_PER_KV, HEAD_DIM)
    k = k.reshape(B, n_chunks, CHUNK, N_KV_HEADS, HEAD_DIM)
    v = v.reshape(B, n_chunks, CHUNK, N_KV_HEADS, HEAD_DIM)

    def band(t):
        parts = [jnp.pad(t, ((0, 0), (j, 0), (0, 0), (0, 0), (0, 0)))[:, :n_chunks]
                 for j in range(WINDOW_CHUNKS - 1, -1, -1)]
        return jnp.concatenate(parts, axis=2)

    kb, vb = band(k), band(v)
    m_len = WINDOW_CHUNKS * CHUNK
    key_chunk = (jnp.arange(n_chunks)[:, None]
                 - (WINDOW_CHUNKS - 1 - jnp.arange(m_len) // CHUNK)[None, :])
    valid = (key_chunk >= 0)[None, :, None, None, None, :]

    scale = 1.0 / math.sqrt(HEAD_DIM)
    s = jnp.einsum('bnqhgd,bnmhd->bnhgqm', q, kb).astype(jnp.float32) * scale
    s = jnp.where(valid, s, jnp.finfo(jnp.float32).min)
    sink = sinks.astype(jnp.float32).reshape(1, 1, N_KV_HEADS, Q_PER_KV, 1)
    m = jnp.maximum(jnp.max(s, axis=-1), sink)
    p = jnp.exp(s - m[..., None])
    denom = jnp.sum(p, axis=-1) + jnp.exp(sink - m)
    p = p / denom[..., None]
    o = jnp.einsum('bnhgqm,bnmhd->bnqhgd', p.astype(v.dtype), vb)
    return o.reshape(B, S, ATTN_WIDTH)

def causal_multiscale_pool(p):
    B, S = p.shape[0], p.shape[1]
    pg = p.reshape(B, S, N_POOL_GROUPS, POOL_GROUP).astype(jnp.float32)
    cs = jnp.cumsum(pg, axis=1)
    means = []
    for gi, w in enumerate(POOL_WINDOWS):
        c_g = cs[:, :, gi]
        lag = jnp.pad(c_g, ((0, 0), (w, 0), (0, 0)))[:, :S]
        count = jnp.minimum(jnp.arange(S) + 1, w).astype(jnp.float32)[None, :, None]
        means.append((c_g - lag) / count)
    mean = jnp.stack(means, axis=2)
    return (mean - pg).astype(p.dtype)

def peer_ffn(h, w_query, sub_keys, expert_down, expert_up):
    B, S, D = h.shape
    n_tok = B * S
    hf = h.reshape(n_tok, D)
    q = (hf @ w_query).reshape(n_tok, PEER_HEADS, 2, PEER_HALF)
    s = jnp.einsum('nhpd,hpkd->nhpk', q, sub_keys).astype(jnp.float32)
    sv, si = lax.top_k(s, PEER_TOPK)
    cand = (sv[:, :, 0, :, None] + sv[:, :, 1, None, :]).reshape(n_tok, PEER_HEADS, PEER_TOPK * PEER_TOPK)
    cidx = (si[:, :, 0, :, None] * N_KEYS + si[:, :, 1, None, :]).reshape(n_tok, PEER_HEADS, PEER_TOPK * PEER_TOPK)
    top, pos = lax.top_k(cand, PEER_TOPK)
    idx = jnp.take_along_axis(cidx, pos, axis=-1)
    gate = jax.nn.softmax(top, axis=-1)

    n_blk = n_tok // PEER_TOKEN_BLOCK

    def block(args):
        hb, ib, gb = args
        u = expert_down[ib]
        a = jnp.einsum('td,thkd->thk', hb, u).astype(jnp.float32)
        act = (jax.nn.gelu(a, approximate=False) * gb).astype(hb.dtype)
        vv = expert_up[ib]
        return jnp.einsum('thk,thkd->td', act, vv)

    out = lax.map(block, (hf.reshape(n_blk, PEER_TOKEN_BLOCK, D),
                          idx.reshape(n_blk, PEER_TOKEN_BLOCK, PEER_HEADS, PEER_TOPK),
                          gate.reshape(n_blk, PEER_TOKEN_BLOCK, PEER_HEADS, PEER_TOPK)))
    return out.reshape(B, S, D)

def setup_inputs(seed: int = 0) -> dict:
    key = jax.random.key(seed)
    ks = jax.random.split(key, 20)
    f32 = jnp.float32
    L, D = DEPTH, D_MODEL

    def nrm(k, shape, scale):
        return jax.random.normal(k, shape, f32) * scale

    return {
        "x": nrm(ks[0], (BATCH, SEQ, D), 1.0),
        "c": nrm(ks[1], (BATCH, D), 1.0),
        "w_ada": nrm(ks[2], (L, D, N_MOD * D), 0.5 * D ** -0.5),
        "b_ada": nrm(ks[3], (L, N_MOD * D), 0.01),
        "norm1_g": 1.0 + nrm(ks[4], (L, D), 0.05),
        "w_in": nrm(ks[5], (L, D, IN_WIDTH), D ** -0.5),
        "q_norm_g": 1.0 + nrm(ks[6], (L, HEAD_DIM), 0.05),
        "k_norm_g": 1.0 + nrm(ks[7], (L, HEAD_DIM), 0.05),
        "attn_sinks": nrm(ks[8], (L, N_Q_HEADS), 1.0),
        "pool_group_w": nrm(ks[9], (L, N_POOL_GROUPS, POOL_GROUP, POOL_GROUP), POOL_GROUP ** -0.5),
        "pool_scale": 1.0 + nrm(ks[10], (L, POOL_WIDTH), 0.1),
        "w_branch_attn": nrm(ks[11], (L, ATTN_WIDTH, D), ATTN_WIDTH ** -0.5),
        "w_branch_pool": nrm(ks[12], (L, POOL_WIDTH, D), POOL_WIDTH ** -0.5),
        "w_out": nrm(ks[13], (L, D, D), D ** -0.5),
        "norm2_g": 1.0 + nrm(ks[14], (L, D), 0.05),
        "w_query": nrm(ks[15], (L, D, PEER_HEADS * PEER_QUERY_DIM), D ** -0.5),
        "sub_keys": nrm(ks[16], (L, PEER_HEADS, 2, N_KEYS, PEER_HALF), PEER_HALF ** -0.5),
        "expert_down": nrm(ks[17], (L, N_EXPERTS, D), D ** -0.5),
        "expert_up": nrm(ks[18], (L, N_EXPERTS, D), (PEER_HEADS * PEER_TOPK) ** -0.5),
    }

def reference(x, c, w_ada, b_ada, norm1_g, w_in, q_norm_g, k_norm_g, attn_sinks,
              pool_group_w, pool_scale, w_branch_attn, w_branch_pool, w_out,
              norm2_g, w_query, sub_keys, expert_down, expert_up):
    B, S, D = x.shape
    cond = jax.nn.silu(c)
    o_q = ATTN_WIDTH
    o_k = o_q + KV_WIDTH
    o_v = o_k + KV_WIDTH
    o_p = o_v + POOL_WIDTH
    o_ga = o_p + D_MODEL
    for l in range(DEPTH):
        mod = cond @ w_ada[l] + b_ada[l]
        shift1, scale1, gate1, shift2, scale2, gate2 = jnp.split(mod, N_MOD, axis=-1)

        h = modulate(rms_norm(x, norm1_g[l]), shift1, scale1)
        z = h @ w_in[l]
        q = rms_norm(z[..., :o_q].reshape(B, S, N_Q_HEADS, HEAD_DIM), q_norm_g[l])
        k = rms_norm(z[..., o_q:o_k].reshape(B, S, N_KV_HEADS, HEAD_DIM), k_norm_g[l])
        v = z[..., o_k:o_v].reshape(B, S, N_KV_HEADS, HEAD_DIM)
        p_in = z[..., o_v:o_p]
        gate_attn = jax.nn.sigmoid(z[..., o_p:o_ga])
        gate_pool = jax.nn.sigmoid(z[..., o_ga:])

        y_attn = chunk_window_attention(q, k, v, attn_sinks[l])
        pooled = causal_multiscale_pool(p_in)
        y_pool = (jnp.einsum('bsgc,gcd->bsgd', pooled, pool_group_w[l]).reshape(B, S, POOL_WIDTH)
                  * pool_scale[l])

        merged = gate_attn * (y_attn @ w_branch_attn[l]) + gate_pool * (y_pool @ w_branch_pool[l])
        x = x + gate1[:, None, :] * (merged @ w_out[l])

        h2 = modulate(rms_norm(x, norm2_g[l]), shift2, scale2)
        x = x + gate2[:, None, :] * peer_ffn(h2, w_query[l], sub_keys[l], expert_down[l], expert_up[l])
    return x


_drawn_inputs = setup_inputs


def setup_inputs(seed=0):
    import zlib

    import numpy as np

    out = dict(_drawn_inputs(seed))
    spreads = {}
    factors = {'b_ada': 8.0,
     'norm1_g': 6.721,
     'q_norm_g': 8.0,
     'k_norm_g': 8.0,
     'attn_sinks': 8.0,
     'pool_scale': 3.853,
     'norm2_g': 8.0,
     'w_query': 3.842,
     'sub_keys': 3.865,
     'expert_down': 4.283,
     'expert_up': 3.845}
    for name, (base, spread) in spreads.items():
        noise = np.random.default_rng([zlib.crc32(name.encode()), seed]).standard_normal(out[name].shape)
        drawn = base * np.exp(spread * noise) if base else spread * noise
        out[name] = __import__('jax').numpy.asarray(drawn.astype(out[name].dtype))
    for name, factor in factors.items():
        out[name] = (out[name] * factor).astype(out[name].dtype)
    return out
```

```python
from contextlib import ExitStack

import concourse.bass as bass
from concourse import mybir

F32 = mybir.dt.float32
F32R = mybir.dt.float32r
U32 = mybir.dt.uint32
ALU = mybir.AluOpType
ACT = mybir.ActivationFunctionType
AX = mybir.AxisListType

P = 128


def build(nc, x, c, w_ada, b_ada, norm1_g, w_in, q_norm_g, k_norm_g, attn_sinks, pool_group_w,
          pool_scale, w_branch_attn, w_branch_pool, w_out, norm2_g, w_query, sub_keys,
          expert_down, expert_up, out):
    _, T, D = x.shape
    C = D // P
    TB = T // P
    HD = q_norm_g.shape[1]
    NQ = attn_sinks.shape[1]
    CHUNK = 64
    AW = w_branch_attn.shape[1]
    PW = w_branch_pool.shape[1]
    QC, PC = AW // P, PW // P
    NG, PG = pool_group_w.shape[1], pool_group_w.shape[2]
    WINDOWS = tuple(2 << g for g in range(NG))
    PH, NK = sub_keys.shape[1], sub_keys.shape[3]
    HP = 2 * PH
    TOPK = 16
    E = expert_down.shape[1]
    EB = E // P
    NKV = (w_in.shape[2] - AW - PW - 2 * D) // 2 // HD
    EPS = 1e-6
    SCALE = float(HD) ** -0.5
    NEG = -3.0e38
    assert C == 16 and TB == 4 and HD == 64 and NQ == 16 and NKV == 2 and NK == P and PG == 2 * P
    assert E == NK * NK and PC == C // 2 and QC == C // 2 and NG == TB

    U_K, U_V, U_POOL = QC, QC + 1, QC + 2
    U_MIX = U_POOL + PC
    U_OUT = U_MIX + 3 * C
    U_QRY = U_OUT + C
    U_END = U_QRY + HP

    xt_dram = nc.dram_tensor("xt_scratch", [C, P, T], F32).ap()
    merged_dram = nc.dram_tensor("merged_scratch", [C, P, T], F32).ap()
    ypool_dram = nc.dram_tensor("ypool_scratch", [PC, P, T], F32).ap()
    x1_dram = nc.dram_tensor("x1_scratch", [C, P, T], F32).ap()
    act_dram = nc.dram_tensor("act_scratch", [EB, P, T], F32).ap()
    gate_dram = nc.dram_tensor("gate_scratch", [EB, P, T], F32).ap()

    def chunked(w):
        return w.rearrange("(c p) n -> p c n", p=P)

    w_ada_v, w_in_v, w_out_v, w_query_v = (chunked(w[0]) for w in (w_ada, w_in, w_out, w_query))
    wba_v, wbp_v = chunked(w_branch_attn[0]), chunked(w_branch_pool[0])
    out_v = out[0]

    ctx = ExitStack()
    with ctx:
        def sem(name):
            return ctx.enter_context(nc.semaphore(name))

        BASE = 16512
        KB = 1024
        END = 229368

        def at(name, shape, dt, off):
            size = 4
            for n in shape[1:]:
                size *= n
            assert BASE + off + size <= END, (name, off, size)
            return nc.alloc_sbuf_tensor_at(name, shape, dt, offset=BASE + off)

        cur = [0]

        def const(name, shape, dt=F32):
            t = at(name, shape, dt, cur[0])
            size = 4
            for n in shape[1:]:
                size *= n
            cur[0] += (size + 31) // 32 * 32
            return t

        ident = const("ident", [P, P])
        ones = const("ones", [P, P])
        blockones = const("blockones", [P, P])
        iota_keys = const("iota_keys", [P, P])
        vec_a = const("vec_a", [P, P])
        vec_b = const("vec_b", [P, 32])
        cond = const("cond", [P, C])
        mod = const("mod", [P, 6 * C])
        mul1 = const("mul1", [P, C])
        mul2 = const("mul2", [P, C])
        eps = const("eps", [P, 1])
        sinks = const("sinks", [P, NQ])
        rcount = const("rcount", [P, NG, 16])
        macc = const("macc", [P, 2, P])
        assert cur[0] <= 6 * KB

        o = 6 * KB
        raw = [at(f"raw{s}", [P, C, P], F32, o + 8 * KB * s) for s in range(2)]
        w_hi_t = [at(f"w_hi{s}", [P, C, P], F32R, o + 8 * KB * (2 + s)) for s in range(2)]
        w_lo_t = [at(f"w_lo{s}", [P, C, P], F32R, o + 8 * KB * (4 + s)) for s in range(2)]
        A0 = o + 48 * KB
        act_hi = at("act_hi", [P, C, T], F32R, A0)
        act_lo = at("act_lo", [P, C, T], F32R, A0 + 32 * KB)
        L0 = A0 + 64 * KB

        MOD_W = 2 * P
        mraw = [at(f"mraw{s}", [P, C, MOD_W], F32, A0 + 16 * KB * s) for s in range(3)]
        xt = at("xt", [P, C, T], F32, L0)
        xrow = [at(f"xrow{s}", [P, D], F32, L0 + 32 * KB + 8 * KB * s) for s in range(2)]
        sq = [at(f"sq{s}", [P, T], F32, L0 + 48 * KB + 2 * KB * s) for s in range(2)]
        rstd = at("rstd", [P, T], F32, L0 + 52 * KB)
        hfull = [at(f"hfull{s}", [P, T], F32, L0 + 54 * KB + 2 * KB * s) for s in range(2)]
        macc_e = [at(f"macc_e{s}", [P, 2, MOD_W], F32, L0 + 58 * KB + 2 * KB * s) for s in range(2)]
        vrow_a = at("vrow_a", [P, P], F32, L0 + 62 * KB)
        vrow_b = at("vrow_b", [P, P], F32, L0 + 62 * KB + 512)
        sinkrow = at("sinkrow", [P, NQ], F32, L0 + 63 * KB)
        csig = at("csig", [P, C], F32, L0 + 63 * KB + 64)

        B0 = L0 + 32 * KB
        kt = at("kt", [P, T], F32, L0 + 64 * KB)
        kdup = [at(f"kdup{k}", [P, T], F32, L0 + 66 * KB + 2 * KB * k) for k in range(NKV)]
        vt = at("vt", [P, T], F32, L0 + 70 * KB)
        vrows = at("vrows", [P, TB, P], F32, L0 + 72 * KB)
        sq2 = [at(f"sqb{s}", [P, T], F32, L0 + 74 * KB + 2 * KB * s) for s in range(2)]
        rq = [at(f"rq{s}", [P, T], F32, L0 + 78 * KB + 2 * KB * s) for s in range(2)]
        qt = at("qt", [P, QC, T], F32, B0)
        y_hi = at("y_hi", [P, QC, T], F32R, B0)
        y_lo = at("y_lo", [P, QC, T], F32R, L0)
        sprob = at("sprob", [P, 4, 2 * P], F32, L0 + 16 * KB)
        prob = at("prob", [P, 4, 2 * P], F32, L0 + 20 * KB)
        prob_t = at("prob_t", [P, 4, 2, P], F32, L0 + 24 * KB)
        stat = at("stat", [P, 6, 4], F32, L0 + 28 * KB)
        PAD = 16
        pin = at("pin", [P, PAD + T], F32, L0 + 48 * KB)
        pwin = [at(f"pwin{s}", [P, PAD + T], F32, L0 + 50 * KB + 256 + (2 * KB + 256) * s) for s in range(2)]
        pooled = at("pooled", [P, 2, T], F32, L0 + 56 * KB)
        pgw = at("pgw", [P, 2, PG], F32, L0 + 60 * KB)
        ypout = at("ypout", [P, T], F32, L0 + 62 * KB)

        yp_hi = at("yp_hi", [P, PC, T], F32R, L0 + 16 * KB)
        assert B0 == L0 + 32 * KB
        yp_lo = at("yp_lo", [P, PC, T], F32R, L0 + 48 * KB)
        mlraw = at("mlraw", [P, C, P], F32, L0 + 64 * KB)
        ypin = at("ypin", [P, T], F32, L0 + 72 * KB)
        sga = at("sga", [P, T], F32, L0 + 74 * KB)
        sgp = at("sgp", [P, T], F32, L0 + 76 * KB)
        mout = [at(f"mout{s}", [P, T], F32, L0 + 78 * KB + 2 * KB * s) for s in range(2)]
        mtmp = at("mtmp", [P, T], F32, L0 + 82 * KB)

        x1t = at("x1t", [P, C, T], F32, L0)
        s_all = at("s_all", [P, TB, HP, NK], F32, L0 + 32 * KB)
        skrow = at("skrow", [P, HP, P], F32, L0 + 32 * KB)
        skt = at("skt", [P, HP, NK], F32, L0 + 72 * KB)
        mgin = [at(f"mgin{s}", [P, T], F32, L0 + 40 * KB + 2 * KB * s) for s in range(2)]
        xtin = [at(f"xtin{s}", [P, T], F32, L0 + 44 * KB + 2 * KB * s) for s in range(2)]
        x1c = [at(f"x1c{s}", [P, T], F32, L0 + 48 * KB + 2 * KB * s) for s in range(2)]
        sq3 = [at(f"sqd{s}", [P, T], F32, L0 + 52 * KB + 2 * KB * s) for s in range(2)]
        rstd2 = at("rstd2", [P, T], F32, L0 + 56 * KB)
        h2full = [at(f"h2full{s}", [P, T], F32, L0 + 58 * KB + 2 * KB * s) for s in range(2)]
        qsb = [at(f"qsb{s}", [P, T], F32, L0 + 80 * KB + 2 * KB * s) for s in range(2)]

        aout = [at(f"aout{s}", [P, T], F32, L0 + 64 * KB + 2 * KB * s) for s in range(2)]
        top_all = at("top_all", [P, TB, PH * TOPK], F32, L0 + 68 * KB)
        i_all = at("i_all", [P, TB, PH * TOPK], F32, L0 + 70 * KB)
        j_all = at("j_all", [P, TB, PH * TOPK], F32, L0 + 72 * KB)
        gate_t = at("gate_t", [P, T], F32, L0 + 74 * KB)
        i_t = at("i_t", [P, T], F32, L0 + 76 * KB)
        j_t = at("j_t", [P, T], F32, L0 + 78 * KB)
        t0 = L0 + 6 * KB
        srow = at("srow", [P, 2, NK], F32, t0)
        srow2 = at("srow2", [P, 2, NK], F32, t0 + KB)
        val = at("val", [P, 2, TOPK], F32, t0 + 2 * KB)
        idx = at("idx", [P, 2, TOPK], U32, t0 + 2 * KB + 128)
        idxf = at("idxf", [P, 2, TOPK], F32, t0 + 2 * KB + 256)
        pos = at("pos", [P, TOPK], U32, t0 + 2 * KB + 384)
        posab = at("posab", [P, 2, TOPK], U32, t0 + 2 * KB + 448)
        posf = at("posf", [P, 2, TOPK], F32, t0 + 2 * KB + 576)
        topv = at("topv", [P, TOPK], F32, t0 + 2 * KB + 704)
        cand = at("cand", [P, TOPK, TOPK], F32, t0 + 3 * KB)
        cand2 = at("cand2", [P, TOPK, TOPK], F32, t0 + 4 * KB)
        pick = at("pick", [P, 2, TOPK, TOPK], F32, t0 + 5 * KB)
        pick2 = at("pick2", [P, 2, TOPK, TOPK], F32, t0 + 7 * KB)
        zsum = at("zsum", [P, TB * PH], F32, t0 + 9 * KB)
        GT = 64
        gbuf = [at(f"gbuf{s}", [P, EB, GT], F32, L0 + 32 * KB * s) for s in range(2)]
        oh_j = [at(f"oh_j{s}", [P, 4, P], F32, A0 + 0 * KB) if False else None for s in range(2)]
        oh_j = at("oh_j", [P, 4, P], F32, L0 + 80 * KB)
        oh_i = at("oh_i", [P, 4, P], F32, L0 + 82 * KB)

        HALF = D // 2
        HC = HALF // P
        up_raw = [at(f"up_raw{s}", [P, HALF], F32, o + 4 * KB * s) for s in range(2)]
        up_hi = [at(f"up_hi{s}", [P, HALF], F32R, o + 8 * KB + 4 * KB * s) for s in range(2)]
        up_lo = [at(f"up_lo{s}", [P, HALF], F32R, o + 16 * KB + 4 * KB * s) for s in range(2)]
        a_in = [at(f"a_in{s}", [P, T], F32, A0 + 2 * KB * s) for s in range(2)]
        g_in = [at(f"g_in{s}", [P, T], F32, A0 + 4 * KB + 2 * KB * s) for s in range(2)]
        ag = [at(f"ag{s}", [P, T], F32, A0 + 8 * KB + 2 * KB * s) for s in range(2)]
        ag_hi = [at(f"ag_hi{s}", [P, T], F32R, A0 + 12 * KB + 2 * KB * s) for s in range(2)]
        ag_lo = [at(f"ag_lo{s}", [P, T], F32R, A0 + 16 * KB + 2 * KB * s) for s in range(2)]
        x1f = at("x1f", [P, C, T], F32, L0)
        orow = [at(f"orow{s}", [P, D], F32, L0 + 32 * KB + 8 * KB * s) for s in range(4)]

        bank = [ctx.enter_context(nc.psum_tensor(f"bank{b}", [P, T], F32)) for b in range(8)]
        B_MOD, B_SUM = bank[7], bank[6]

        raw_landed = [sem(f"raw_landed{s}") for s in range(2)]
        raw_seen = sem("raw_seen")
        hi_ready = sem("hi_ready")
        lo_ready = sem("lo_ready")
        unit_done = sem("unit_done")
        z_free = [sem(f"z_free{s}") for s in range(2)]

        def load_unit(sp, u, *parts):
            s = slot(u)
            if not (isinstance(u, int) and u < 2):
                sp.wait_ge(lo_ready, u - 1)
            if len(parts) == 1:
                sp.dma_start(raw[s][:, :, :], parts[0]).then_inc(raw_landed[s], 16)
            else:
                half = C // 2
                sp.sem_inc(raw_seen, 1)
                sp.dma_start(raw[s][:, 0:half, :], parts[0]).then_inc(raw_landed[s], 16)
                sp.dma_start(raw[s][:, half:C, :], parts[1]).then_inc(raw_landed[s], 16)

        parity = {}

        def unit(base, i, step, off):
            u = base + step * i + off
            parity[id(u)] = (u, (base + off) % 2)
            return u

        def slot(u):
            return u % 2 if isinstance(u, int) else parity[id(u)][1]

        def landed(u):
            return u

        def split_hi(act, u, count):
            s = slot(u)
            act.wait_ge(raw_landed[s], 16 * count)
            if not (isinstance(u, int) and u < 2):
                act.wait_ge(unit_done, u - 1)
            act.activation(w_hi_t[s][:, :, :], raw[s][:, :, :], ACT.Copy).then_inc(hi_ready, 1)

        def split_lo(dve, u):
            s = slot(u)
            dve.wait_ge(hi_ready, u + 1)
            dve.tensor_tensor(w_lo_t[s][:, :, :], raw[s][:, :, :], w_hi_t[s][:, :, :].bitcast(F32),
                              ALU.subtract).then_inc(lo_ready, 1)

        def three_pass(pe, dst, s, cw, mh, ml, first, last):
            pe.matmul(dst, w_hi_t[s][:, cw, :], mh, start=first, stop=False)
            pe.matmul(dst, w_hi_t[s][:, cw, :], ml, start=False, stop=False)
            return pe.matmul(dst, w_lo_t[s][:, cw, :], mh, start=False, stop=last)

        def lands(u0):
            n = 0
            for u in range(u0 % 2, u0 + 1, 2):
                n += 2 if U_MIX <= u < U_OUT and (u - U_MIX) % 3 == 2 else 1
            return n

        def lands_in(base, i, step, off):
            a = lands(base + off)
            b = lands(base + off + step)
            return a + (b - a) * i

        io = sem("vectors_landed")
        consts = sem("consts")
        pool_step = sem("pool_step")
        vec_t = sem("vec_t")
        vec_c = sem("vec_c")
        cond_ready = sem("cond_ready")
        mraw_landed = [sem(f"mraw_landed{s}") for s in range(2)]
        mstep = sem("mstep")
        macc_ready = sem("macc_ready")
        msum_done = sem("msum_done")
        mod_ready = sem("mod_ready")
        x_landed = [sem(f"x_landed{s}") for s in range(2)]
        xtr_done = sem("xtr_done")
        xt_copied = sem("xt_copied")
        xt_stored = sem("xt_stored")
        sq_ready = sem("sq_ready")
        ss_step = sem("ss_step")
        rms_root = sem("rms_root")
        rms_ready = sem("rms_ready")
        xn_ready = sem("xn_ready")

        mix_free = sem("mix_free")
        ml_done = sem("ml_done")
        ml_evac = sem("ml_evac")
        g_done = sem("g_done")
        a_stored = [sem(f"a_stored{s}") for s in range(2)]
        g_stored = [sem(f"g_stored{s}") for s in range(2)]

        NE = 2 * C // 2

        with nc.Block() as block:
            @block.gpsimd
            def _(pool):
                for free in (ml_done, ml_evac, mix_free, g_done):
                    pool.sem_inc(free, 1)
                for s in range(2):
                    pool.sem_inc(a_stored[s], 16)
                pool.memset(ones[:, :], 1.0).then_inc(pool_step, 1)
                pool.memset(ident[:, :], 0.0).then_inc(pool_step, 1)
                pool.memset(blockones[:, :], 0.0).then_inc(pool_step, 1)
                pool.memset(eps[:, :], EPS).then_inc(pool_step, 1)
                pool.wait_ge(pool_step, 4)
                pool.affine_select(out=ident[:, :], in_=ident[:, :], compare_op=ALU.not_equal, fill=1.0,
                                   base=0, pattern=[[-1, P]], channel_multiplier=1).then_inc(consts, 1)
                pool.wait_ge(consts, 1)
                pool.memset(blockones[0:HD, 0:HD], 1.0).then_inc(consts, 1)
                pool.wait_ge(consts, 2)
                pool.memset(blockones[HD:P, HD:P], 1.0).then_inc(consts, 1)
                pool.wait_ge(consts, 3)
                pool.iota(iota_keys[:, :], pattern=[[1, P]], base=0, channel_multiplier=0,
                          allow_small_or_imprecise_dtypes=True).then_inc(consts, 1)
                for g, w in enumerate(WINDOWS):
                    for t in range(16):
                        if t < w - 1:
                            pool.memset(rcount[:, g, t:t + 1], 1.0 / (t + 1)).then_inc(consts, 1)
                    pool.memset(rcount[:, g, w - 1:16], 1.0 / w).then_inc(consts, 1)

            @block.sync
            def _(sp):
                sp.dma_start(vrow_a[0:6 * C, :], b_ada[0].rearrange("(r p) -> r p", p=P)).then_inc(io, 16)
                sp.dma_start(vrow_a[6 * C:7 * C, :], c[0].rearrange("(r p) -> r p", p=P)).then_inc(io, 16)
                sp.dma_start(vrow_a[7 * C:8 * C, :], norm1_g[0].rearrange("(r p) -> r p", p=P)).then_inc(io, 16)
                sp.dma_start(vrow_b[0:C, :], norm2_g[0].rearrange("(r p) -> r p", p=P)).then_inc(io, 16)
                sp.dma_start(vrow_b[C:C + PC, :], pool_scale[0].rearrange("(r p) -> r p", p=P)).then_inc(io, 16)
                for k in range(2):
                    sp.dma_start(vrow_b[C + PC:C + PC + 1, k * HD:(k + 1) * HD], q_norm_g).then_inc(io, 16)
                    sp.dma_start(vrow_b[C + PC + 1:C + PC + 2, k * HD:(k + 1) * HD], k_norm_g).then_inc(io, 16)
                sp.dma_start(sinkrow[0:1, :], attn_sinks).then_inc(io, 16)
                for tb in range(2):
                    sp.dma_start(xrow[tb][:, :], x[0, tb * P:(tb + 1) * P, :]).then_inc(x_landed[tb], 16)
                for s in range(2):
                    sp.dma_start(mraw[s][:, :, :], w_ada_v[:, :, s * MOD_W:(s + 1) * MOD_W])\
                      .then_inc(mraw_landed[s], 16)
                for tb in range(2, TB):
                    sp.wait_ge(xtr_done, 4 * (tb - 1))
                    sp.dma_start(xrow[tb % 2][:, :], x[0, tb * P:(tb + 1) * P, :])\
                      .then_inc(x_landed[tb % 2], 16)
                load_unit(sp, 0, w_in_v[:, :, 0:P])
                load_unit(sp, 1, w_in_v[:, :, P:2 * P])
                with sp.Fori(1, NE // 2) as i:
                    for s in range(2):
                        sp.wait_ge(macc_ready, 2 * i + s - 1)
                        sp.dma_start(mraw[s][:, :, :],
                                     w_ada_v[:, :, bass.ds((2 * i + s) * MOD_W, MOD_W)])\
                          .then_inc(mraw_landed[s], 16)
                sp.wait_ge(xt_copied, 4 * TB)
                sp.dma_start(xt_dram.rearrange("c p t -> p c t"), xt[:, :, :]).then_inc(xt_stored, 16)
                sp.wait_ge(xt_stored, 16)

            @block.tensor
            def _(pe):
                pe.wait_ge(consts, 1)
                pe.wait_ge(io, 16 * 10)
                pe.transpose(bank[0][:, 0:P], vrow_a[:, :], ident[:, :])
                pe.transpose(bank[0][:, P:P + 26], vrow_b[0:26, :], ident[0:26, 0:26])
                pe.matmul(bank[0][:, 2 * P:2 * P + NQ], ones[0:1, :], sinkrow[0:1, :],
                          start=True, stop=True).then_inc(vec_t, 1)
                pe.wait_ge(vec_c, 1)
                for tb in range(TB):
                    pe.wait_ge(x_landed[tb % 2], 16 * (tb // 2 + 1))
                    for q in range(4):
                        if tb:
                            pe.wait_ge(xt_copied, 4 * (tb - 1) + q + 1)
                        for r in range(4):
                            cc = 4 * q + r
                            mm = pe.transpose(bank[q][:, r * P:(r + 1) * P],
                                              xrow[tb % 2][:, cc * P:(cc + 1) * P], ident[:, :])
                        mm.then_inc(xtr_done, 1)
                for cc in range(C):
                    pe.wait_ge(sq_ready, cc + 1)
                    pe.matmul(B_SUM[:, :], ones[:, :], sq[cc % 2][:, :], start=(cc == 0),
                              stop=(cc == C - 1)).then_inc(ss_step, 1)
                with pe.Fori(0, NE // 2) as i:
                    for s in range(2):
                        pe.wait_ge(macc_ready, 2 * i + s + 1)
                        pe.wait_ge(mod_ready, 2 * i + s + 1)
                        for k in range(2):
                            for e in range(2):
                                mm = pe.matmul(B_MOD[:, k:k + 1], macc_e[s][:, e, k * P:(k + 1) * P],
                                               ones[:, 0:1], start=(e == 0), stop=(e == 1))
                        mm.then_inc(msum_done, 1)

            @block.scalar
            def _(act):
                act.wait_ge(vec_c, 1)
                act.activation(csig[:, :], vec_a[:, 6 * C:7 * C], ACT.Sigmoid).then_inc(vec_c, 1)
                for tb in range(TB):
                    for q in range(4):
                        act.wait_ge(xtr_done, 4 * tb + q + 1)
                        act.activation(xt[:, 4 * q:4 * q + 4, tb * P:(tb + 1) * P],
                                       bank[q][:, :].rearrange("p (r t) -> p r t", r=4),
                                       ACT.Copy).then_inc(xt_copied, 1)
                act.wait_ge(xt_copied, 4 * TB)
                for cc in range(C):
                    if cc >= 2:
                        act.wait_ge(ss_step, cc - 1)
                    act.activation(sq[cc % 2][:, :], xt[:, cc, :], ACT.Square).then_inc(sq_ready, 1)
                act.wait_ge(ss_step, C)
                act.activation(rstd[:, :], B_SUM[:, :], ACT.Sqrt, bias=eps[:, :], scale=1.0 / D)\
                   .then_inc(rms_root, 1)
                split_hi(act, 0, 1)
                split_hi(act, 1, 1)

            @block.vector
            def _(dve):
                dve.sem_inc(mod_ready, 1)
                dve.wait_ge(vec_t, 1)
                dve.tensor_copy(vec_a[:, :], bank[0][:, 0:P])
                dve.tensor_copy(vec_b[:, 0:26], bank[0][:, P:P + 26])
                dve.tensor_copy(sinks[:, :], bank[0][:, 2 * P:2 * P + NQ]).then_inc(vec_c, 1)
                dve.wait_ge(vec_c, 2)
                dve.tensor_tensor(cond[:, :], vec_a[:, 6 * C:7 * C], csig[:, :], ALU.mult)\
                   .then_inc(cond_ready, 1)
                dve.wait_ge(cond_ready, 1)

                def early(i, s):
                    v = 2 * i + s
                    if not (isinstance(i, int) and i == 0):
                        dve.wait_ge(msum_done, v - 1)
                    dve.wait_ge(mraw_landed[s], 16 * (i + 1))
                    for cc in range(C):
                        e = cc % 2
                        if cc < 2:
                            ins = dve.tensor_scalar(macc_e[s][:, e, :], mraw[s][:, cc, :],
                                                    cond[:, cc:cc + 1], None, ALU.mult)
                        else:
                            dve.wait_ge(mstep, C * v + cc - 1)
                            ins = dve.scalar_tensor_tensor(
                                out=macc_e[s][:, e, :], in0=mraw[s][:, cc, :], scalar=cond[:, cc:cc + 1],
                                in1=macc_e[s][:, e, :], op0=ALU.mult, op1=ALU.add)
                        ins.then_inc(mstep, 1)
                    dve.wait_ge(mstep, C * v + C)
                    dve.sem_inc(macc_ready, 1)
                    dve.wait_ge(msum_done, v + 1)
                    dve.tensor_tensor(mod[:, bass.ds(2 * v, 2)], B_MOD[:, 0:2], vec_a[:, bass.ds(2 * v, 2)],
                                      ALU.add).then_inc(mod_ready, 1)

                early(0, 0)
                early(0, 1)
                with dve.Fori(1, NE // 2) as i:
                    early(i, 0)
                    early(i, 1)
                dve.wait_ge(rms_root, 1)
                dve.reciprocal(rstd[:, :], rstd[:, :]).then_inc(rms_ready, 1)
                dve.wait_ge(rms_ready, 1)
                dve.wait_ge(xt_stored, 16)
                for cc in range(C):
                    dve.tensor_tensor(xt[:, cc, :], xt[:, cc, :], rstd[:, :], ALU.mult)\
                       .then_inc(xn_ready, 1)
                dve.wait_ge(mod_ready, NE + 1)
                dve.scalar_tensor_tensor(out=mul1[:, :], in0=mod[:, C:2 * C], scalar=1.0,
                                         in1=vec_a[:, 7 * C:8 * C], op0=ALU.add, op1=ALU.mult)\
                   .then_inc(xn_ready, 1)
                split_lo(dve, 0)
                split_lo(dve, 1)

        h_full = sem("h_full")
        h_hi = sem("h_hi")
        h_ready = sem("h_ready")
        zc_ready = sem("zc_ready")
        zq_ready = sem("zq_ready")
        hs_done = sem("hs_done")
        hr_root = sem("hr_root")
        hr_inv = sem("hr_inv")
        qk_ready = sem("qk_ready")
        kdup_landed = sem("kdup_landed")
        vtr_done = sem("vtr_done")
        v_ready = sem("v_ready")
        mask_ready = sem("mask_ready")
        s_done = sem("s_done")
        s_max = sem("s_max")
        s_shift = sem("s_shift")
        s_stat = sem("s_stat")
        s_exp = sem("s_exp")
        s_esink = sem("s_esink")
        s_sum = sem("s_sum")
        p_ready = sem("p_ready")
        pt_done = sem("pt_done")
        pt_copied = sem("pt_copied")
        o_done = sem("o_done")
        y_hi_done = sem("y_hi_done")
        y_ready = sem("y_ready")
        pin_ready = sem("pin_ready")
        win_step = sem("win_step")
        pooled_ready = sem("pooled_ready")
        pgw_landed = sem("pgw_landed")
        pl_done = sem("pl_done")
        yp_ready = sem("yp_ready")
        yp_stored = sem("yp_stored")
        pad_ready = sem("pad_ready")

        def z_uses(u):
            return u // 2

        def z_unit(pe, u, nuse, cs=None, wait_h=False):
            s = slot(u)
            cs = range(C) if cs is None else cs
            if cs[0] == 0:
                pe.wait_ge(lo_ready, u + 1)
                if not (isinstance(nuse, int) and nuse == 0):
                    pe.wait_ge(z_free[s], nuse)
            for cc in cs:
                if wait_h:
                    pe.wait_ge(h_ready, cc + 1)
                mm = three_pass(pe, bank[s][:, :], s, cc, act_hi[:, cc, :], act_lo[:, cc, :],
                                cc == 0, cc == C - 1)
            if cs[-1] == C - 1:
                mm.then_inc(unit_done, 1)

        GROUPS = [(tb, hg) for tb in range(TB) for hg in range(NQ // 4)]

        with nc.Block() as block:
            @block.sync
            def _(sp):
                for u in range(2, U_MIX):
                    load_unit(sp, u, w_in_v[:, :, u * P:(u + 1) * P])
                    if u == U_POOL + 1:
                        sp.wait_ge(qk_ready, QC + 1)
                        for k in range(NKV):
                            for half in range(2):
                                sp.dma_start(kdup[k][half * HD:(half + 1) * HD, :],
                                             kt[k * HD:(k + 1) * HD, :]).then_inc(kdup_landed, 16)
                for u in range(U_MIX, U_MIX + 2):
                    off = AW + 2 * NKV * HD + PW + (u - U_MIX) * D
                    load_unit(sp, u, w_in_v[:, :, off:off + P])

            @block.tensor
            def _(pe):
                def head_sums(j):
                    pe.wait_ge(zq_ready, j + 1)
                    if j:
                        pe.wait_ge(hr_root, j)
                    pe.matmul(B_SUM[:, :], blockones[:, :], sq2[j % 2][:, :], start=True, stop=True)\
                      .then_inc(hs_done, 1)

                for u in range(U_POOL):
                    z_unit(pe, u, z_uses(u), wait_h=(u == 0))
                    if 1 <= u <= U_K + 1:
                        head_sums(u - 1)
                pe.wait_ge(zc_ready, U_V + 1)
                pe.wait_ge(hr_root, U_K + 1)
                for tb in range(TB):
                    mm = pe.transpose(bank[7][:, tb * P:(tb + 1) * P], vt[:, tb * P:(tb + 1) * P], ident[:, :])
                mm.then_inc(vtr_done, 1)

                def scores(n):
                    tb, hg = GROUPS[n]
                    if n == 0:
                        pe.wait_ge(qk_ready, QC + 1)
                        pe.wait_ge(kdup_landed, 16 * 2 * NKV)
                    else:
                        pe.wait_ge(s_shift, 2 * n)
                    for r in range(4):
                        h = 4 * hg + r
                        ps = (h % 2) * HD
                        lo = P if tb == 0 else HD
                        mm = pe.matmul(bank[4 + r % 2][:, (r // 2) * 2 * P + lo:(r // 2 + 1) * 2 * P],
                                       qt[ps:ps + HD, h // 2, tb * P:(tb + 1) * P],
                                       kdup[hg // 2][ps:ps + HD, (tb - 1) * P + lo:(tb + 1) * P],
                                       start=True, stop=True)
                    mm.then_inc(s_done, 1)

                def values(n):
                    tb, hg = GROUPS[n]
                    pe.wait_ge(p_ready, n + 1)
                    if n:
                        pe.wait_ge(pt_copied, 2 * n)
                    for b in range(2):
                        for r in range(2):
                            for k in range(2):
                                mm = pe.transpose(bank[2 + b][:, (2 * r + k) * P:(2 * r + k + 1) * P],
                                                  prob[:, 2 * b + r, k * P:(k + 1) * P], ident[:, :])
                        mm.then_inc(pt_done, 1)
                    if n == 0:
                        pe.wait_ge(v_ready, 1)
                    else:
                        pe.wait_ge(y_ready, n)
                    pe.wait_ge(pt_copied, 2 * n + 2)
                    kv = hg // 2
                    for r in range(4):
                        ps = (r // 2) * HD
                        dst = B_SUM[ps:ps + HD, (r % 2) * P:(r % 2 + 1) * P]
                        for k in range(2):
                            if tb == 0 and k == 0:
                                continue
                            mm = pe.matmul(dst, vrows[:, tb - 1 + k, kv * HD:(kv + 1) * HD],
                                           prob_t[:, r, k, :], start=(k == 0 or tb == 0), stop=(k == 1))
                    mm.then_inc(o_done, 1)

                def pool_linear(g):
                    pe.wait_ge(pooled_ready, 2 * g + 2)
                    pe.wait_ge(pgw_landed, 16 * (g + 1))
                    for m in range(2):
                        n = 2 * g + m
                        if n == 0:
                            pe.wait_ge(v_ready, 1)
                        else:
                            pe.wait_ge(yp_ready, n)
                        for k in range(2):
                            mm = pe.matmul(bank[7][:, :], pgw[:, k, m * P:(m + 1) * P], pooled[:, k, :],
                                           start=(k == 0), stop=(k == 1))
                        mm.then_inc(pl_done, 1)

                for p in range(PC):
                    u = U_POOL + p
                    scores(2 * p)
                    z_unit(pe, u, z_uses(u), cs=range(0, C // 2))
                    values(2 * p)
                    scores(2 * p + 1)
                    z_unit(pe, u, z_uses(u), cs=range(C // 2, C))
                    values(2 * p + 1)
                    if p % 2 == 0 and p:
                        pool_linear(p // 2 - 1)
                pool_linear(NG - 1)

            @block.scalar
            def _(act):
                for cc in range(C):
                    act.wait_ge(h_full, cc + 1)
                    act.activation(act_hi[:, cc, :], hfull[cc % 2][:, :], ACT.Copy).then_inc(h_hi, 1)
                for u in range(U_POOL):
                    s = u % 2
                    if u:
                        split_hi(act, u + 1, lands(u + 1))
                    act.wait_ge(unit_done, u + 1)
                    dst = qt[:, u, :] if u < QC else (kt if u == U_K else vt)[:, :]
                    if u <= U_K:
                        act.activation(dst, bank[s][:, :], ACT.Copy).then_inc(zc_ready, 1)
                        if u >= 2:
                            act.wait_ge(hs_done, u - 1)
                        act.activation(sq2[s][:, :], bank[s][:, :], ACT.Square).then_inc(zq_ready, 1)
                        act.wait_ge(zq_ready, u + 1)
                        act.wait_ge(zc_ready, u + 1)
                        act.sem_inc(z_free[s], 1)
                    else:
                        act.activation(dst, bank[s][:, :], ACT.Copy).then_inc(zc_ready, 1)
                        act.wait_ge(zc_ready, u + 1)
                        act.sem_inc(z_free[s], 1)
                    if 1 <= u <= U_K + 1:
                        j = u - 1
                        act.wait_ge(hs_done, j + 1)
                        if j >= 2:
                            act.wait_ge(qk_ready, j - 1)
                        act.activation(rq[j % 2][:, :], B_SUM[:, :], ACT.Sqrt, bias=eps[:, :],
                                       scale=1.0 / HD).then_inc(hr_root, 1)

                def softmax_exp(n):
                    act.wait_ge(s_shift, 2 * n + 2)
                    if n:
                        act.wait_ge(pt_done, 2 * n)
                    act.activation(prob[:, :, :], sprob[:, :, :], ACT.Exp).then_inc(s_exp, 1)
                    act.wait_ge(s_stat, 2 * n + 2)
                    act.activation(stat[:, 3, :], stat[:, 2, :], ACT.Exp).then_inc(s_esink, 1)

                def copy_probs(n):
                    for b in range(2):
                        act.wait_ge(pt_done, 2 * n + b + 1)
                        if n:
                            act.wait_ge(o_done, n)
                        act.activation(prob_t[:, 2 * b:2 * b + 2, :, :],
                                       bank[2 + b][:, :].rearrange("p (r k t) -> p r k t", r=2, k=2),
                                       ACT.Copy).then_inc(pt_copied, 1)

                def y_high(n):
                    tb, hg = GROUPS[n]
                    act.wait_ge(o_done, n + 1)
                    act.activation(y_hi[:, 2 * hg:2 * hg + 2, tb * P:(tb + 1) * P],
                                   B_SUM[:, 0:2 * P].rearrange("p (r t) -> p r t", r=2),
                                   ACT.Copy).then_inc(y_hi_done, 1)

                def pool_in(p):
                    u = U_POOL + p
                    s = u % 2
                    act.wait_ge(unit_done, u + 1)
                    if p:
                        act.wait_ge(pooled_ready, p)
                    else:
                        act.wait_ge(pad_ready, 1)
                    act.activation(pin[:, PAD:], bank[s][:, :], ACT.Copy).then_inc(pin_ready, 1)
                    act.wait_ge(pin_ready, p + 1)
                    act.sem_inc(z_free[s], 1)

                for p in range(PC):
                    u = U_POOL + p
                    softmax_exp(2 * p)
                    split_hi(act, u + 1, lands(u + 1))
                    copy_probs(2 * p)
                    y_high(2 * p)
                    softmax_exp(2 * p + 1)
                    pool_in(p)
                    copy_probs(2 * p + 1)
                    y_high(2 * p + 1)

            @block.vector
            def _(dve):
                for cc in range(C):
                    if cc >= 2:
                        dve.wait_ge(h_ready, cc - 1)
                    dve.wait_ge(xn_ready, C + 1)
                    dve.tensor_scalar(hfull[cc % 2][:, :], xt[:, cc, :], mul1[:, cc:cc + 1],
                                      mod[:, cc:cc + 1], ALU.mult, ALU.add).then_inc(h_full, 1)
                    dve.wait_ge(h_hi, cc + 1)
                    dve.tensor_tensor(act_lo[:, cc, :], hfull[cc % 2][:, :], act_hi[:, cc, :].bitcast(F32),
                                      ALU.subtract).then_inc(h_ready, 1)

                def normalise(j):
                    dve.wait_ge(hr_root, j + 1)
                    dve.reciprocal(rq[j % 2][:, :], rq[j % 2][:, :]).then_inc(hr_inv, 1)
                    dve.wait_ge(hr_inv, j + 1)
                    dve.wait_ge(zc_ready, j + 1)
                    z = qt[:, j, :] if j < QC else kt[:, :]
                    col = C + PC + (j == U_K)
                    dve.scalar_tensor_tensor(out=z, in0=z, scalar=vec_b[:, col:col + 1],
                                             in1=rq[j % 2][:, :], op0=ALU.mult, op1=ALU.mult)\
                       .then_inc(qk_ready, 1)

                for u in range(U_POOL):
                    if u:
                        split_lo(dve, u + 1)
                        if u <= U_K + 1:
                            normalise(u - 1)
                dve.wait_ge(vtr_done, 1)
                dve.tensor_copy(vrows[:, :, :], bank[7][:, :].rearrange("p (b d) -> p b d", b=TB))\
                   .then_inc(v_ready, 1)

                def by_bank(v):
                    return v.rearrange("p (b r) -> p b r", b=2)

                def sinks_of(hg):
                    return sinks[:, 4 * hg:4 * hg + 4].rearrange("p (r b) -> p b r", b=2)

                def softmax_max(n):
                    tb, hg = GROUPS[n]
                    dve.wait_ge(s_done, n + 1)
                    spans = [(0, P if tb == 0 else HD, P + HD), (HD, P, 2 * P)]
                    for half, (ps, lo, hi) in enumerate(spans):
                        for b in range(2):
                            ins = dve.tensor_reduce(
                                stat[ps:ps + HD, 0, 2 * b:2 * b + 2],
                                bank[4 + b][ps:ps + HD, :].rearrange("p (r m) -> p r m", r=2)[:, :, lo:hi],
                                AX.X, ALU.max)
                    ins.then_inc(s_max, 1)
                    dve.wait_ge(s_max, 2 * n + 1)
                    dve.scalar_tensor_tensor(out=by_bank(stat[:, 1, :]), in0=by_bank(stat[:, 0, :]),
                                             scalar=SCALE, in1=sinks_of(hg), op0=ALU.mult, op1=ALU.max)\
                       .then_inc(s_max, 1)
                    dve.wait_ge(s_max, 2 * n + 2)
                    if n:
                        dve.wait_ge(s_exp, n)
                    for b in range(2):
                        for half, (ps, lo, hi) in enumerate(spans):
                            ins = dve.scalar_tensor_tensor(
                                out=sprob[ps:ps + HD, 2 * b:2 * b + 2, lo:hi],
                                in0=bank[4 + b][ps:ps + HD, :].rearrange("p (r m) -> p r m", r=2)[:, :, lo:hi],
                                scalar=SCALE,
                                in1=stat[ps:ps + HD, 1, 2 * b:2 * b + 2].unsqueeze(2).to_broadcast([HD, 2, hi - lo]),
                                op0=ALU.mult, op1=ALU.subtract)
                        ins.then_inc(s_shift, 1)
                    if n:
                        dve.wait_ge(s_esink, n)
                    dve.tensor_tensor(by_bank(stat[:, 2, :]), sinks_of(hg), by_bank(stat[:, 1, :]),
                                      ALU.subtract).then_inc(s_stat, 2)

                def softmax_norm(n):
                    dve.wait_ge(s_exp, n + 1)
                    dve.wait_ge(s_esink, n + 1)
                    dve.tensor_reduce(stat[:, 4, :], prob[:, :, :], AX.X, ALU.add).then_inc(s_sum, 1)
                    dve.wait_ge(s_sum, 3 * n + 1)
                    dve.tensor_tensor(stat[:, 4, :], stat[:, 4, :], stat[:, 3, :], ALU.add).then_inc(s_sum, 1)
                    dve.wait_ge(s_sum, 3 * n + 2)
                    dve.reciprocal(stat[:, 5, :], stat[:, 4, :]).then_inc(s_sum, 1)
                    dve.wait_ge(s_sum, 3 * n + 3)
                    dve.tensor_tensor(prob[:, :, :], prob[:, :, :],
                                      stat[:, 5, :].unsqueeze(2).to_broadcast([P, 4, 2 * P]),
                                      ALU.mult).then_inc(p_ready, 1)

                def y_low(n):
                    tb, hg = GROUPS[n]
                    dve.wait_ge(y_hi_done, n + 1)
                    dve.tensor_tensor(y_lo[:, 2 * hg:2 * hg + 2, tb * P:(tb + 1) * P],
                                      B_SUM[:, 0:2 * P].rearrange("p (r t) -> p r t", r=2),
                                      y_hi[:, 2 * hg:2 * hg + 2, tb * P:(tb + 1) * P].bitcast(F32),
                                      ALU.subtract).then_inc(y_ready, 1)

                def pool_out(g):
                    for m in range(2):
                        n = 2 * g + m
                        dve.wait_ge(pl_done, n + 1)
                        if n:
                            dve.wait_ge(yp_stored, 16 * n)
                        dve.tensor_scalar(ypout[:, :], bank[7][:, :], vec_b[:, C + n:C + n + 1], None,
                                          ALU.mult).then_inc(yp_ready, 1)

                dve.memset(sprob[:, :, :], -1.0e30).then_inc(mask_ready, 1)
                dve.wait_ge(mask_ready, 1)
                for p in range(PC):
                    u = U_POOL + p
                    softmax_max(2 * p)
                    split_lo(dve, u + 1)
                    softmax_norm(2 * p)
                    y_low(2 * p)
                    softmax_max(2 * p + 1)
                    softmax_norm(2 * p + 1)
                    y_low(2 * p + 1)
                    if p % 2 == 0 and p:
                        pool_out(p // 2 - 1)
                pool_out(NG - 1)

            @block.gpsimd
            def _(pool):
                pool.wait_ge(h_ready, C)
                pool.memset(pin[:, 0:PAD], 0.0)
                pool.memset(pwin[0][:, 0:PAD], 0.0)
                pool.memset(pwin[1][:, 0:PAD], 0.0).then_inc(pad_ready, 1)
                def load_linear(g):
                    pool.dma_start(pgw[:, :, :], pool_group_w[0, g].rearrange("(c p) n -> p c n", p=P))\
                        .then_inc(pgw_landed, 16)

                def store_pooled(g):
                    for n in range(2 * g, 2 * g + 2):
                        pool.wait_ge(yp_ready, n + 1)
                        pool.dma_start(ypool_dram[n], ypout[:, :]).then_inc(yp_stored, 16)

                load_linear(0)
                step = 0
                for p in range(PC):
                    g, w = p // 2, WINDOWS[p // 2]
                    if g and p % 2:
                        store_pooled(g - 1)
                        load_linear(g)
                    pool.wait_ge(pin_ready, p + 1)
                    src, k, n = pin, 1, 0
                    while k < w:
                        dst = pwin[n % 2]
                        pool.tensor_tensor(dst[:, PAD:], src[:, PAD:], src[:, PAD - k:PAD - k + T],
                                           ALU.add).then_inc(win_step, 1)
                        step += 1
                        pool.wait_ge(win_step, step)
                        src, k, n = dst, 2 * k, n + 1
                    pool.tensor_tensor(src[:, PAD:PAD + 16], src[:, PAD:PAD + 16], rcount[:, g, :],
                                       ALU.mult).then_inc(win_step, 1)
                    pool.tensor_scalar(src[:, PAD + 16:], src[:, PAD + 16:], 1.0 / w, None,
                                       ALU.mult).then_inc(win_step, 1)
                    step += 2
                    pool.wait_ge(win_step, step)
                    if p >= 2:
                        pool.wait_ge(pl_done, 2 * g)
                    pool.tensor_tensor(pooled[:, p % 2, :], src[:, PAD:], pin[:, PAD:], ALU.subtract)\
                        .then_inc(pooled_ready, 1)
                store_pooled(NG - 1)
                pool.wait_ge(yp_stored, 16 * PC)

        yp_landed = sem("yp_landed")
        yp_hi_done = sem("yp_hi_done")
        yp_halves = sem("yp_halves")
        sig_ready = sem("sig_ready")
        mix_step = sem("mix_step")
        m_ready = sem("m_ready")
        m_stored = [sem(f"m_stored{s}") for s in range(2)]
        ml_landed = sem("ml_landed")
        ml_step = sem("ml_step")
        OFF_GA = AW + 2 * NKV * HD + PW

        def late_sums(dve, v):
            dve.wait_ge(ml_landed, 16 * (v + 1))
            dve.wait_ge(ml_done, v + 1)
            for cc in range(C):
                e = cc % 2
                if cc < 2:
                    ins = dve.tensor_scalar(macc[:, e, :], mlraw[:, cc, :], cond[:, cc:cc + 1], None, ALU.mult)
                else:
                    dve.wait_ge(ml_step, C * v + cc - 1)
                    ins = dve.scalar_tensor_tensor(out=macc[:, e, :], in0=mlraw[:, cc, :],
                                                   scalar=cond[:, cc:cc + 1], in1=macc[:, e, :],
                                                   op0=ALU.mult, op1=ALU.add)
                ins.then_inc(ml_step, 1)

        def late_column(dve, v):
            dve.wait_ge(ml_done, v + 2)
            dve.tensor_tensor(mod[:, bass.ds(2 * C + v, 1)], B_MOD[:, 0:1],
                              vec_a[:, bass.ds(2 * C + v, 1)], ALU.add).then_inc(ml_evac, 1)

        def late_pe(pe, v):
            pe.wait_ge(ml_step, C * v + C)
            pe.wait_ge(ml_evac, v + 1)
            for e in range(2):
                mm = pe.matmul(B_MOD[:, 0:1], macc[:, e, :], ones[:, 0:1], start=(e == 0), stop=(e == 1))
            mm.then_inc(ml_done, 1)

        def late_load(sp, v):
            sp.wait_ge(ml_step, C * v)
            sp.dma_start(mlraw[:, :, :], w_ada_v[:, :, bass.ds((2 * C + v) * P, P)]).then_inc(ml_landed, 16)

        with nc.Block() as block:
            @block.sync
            def _(sp):
                sp.dma_start(mlraw[:, :, :], w_ada_v[:, :, 2 * C * P:(2 * C + 1) * P]).then_inc(ml_landed, 16)
                for n in range(PC):
                    if n:
                        sp.wait_ge(yp_halves, n)
                    sp.dma_start(ypin[:, :], ypool_dram[n]).then_inc(yp_landed, 16)

                def mix_loads(m, first=False):
                    for r in range(2):
                        for k in range(3):
                            off = 3 * r + k
                            u = unit(U_MIX, m, 6, off)
                            if first and off < 2:
                                continue
                            col = (2 * m + r) * P
                            if k < 2:
                                load_unit(sp, u, w_in_v[:, :, bass.ds(OFF_GA + k * D + col, P)])
                            else:
                                load_unit(sp, u, wba_v[:, :, bass.ds(col, P)], wbp_v[:, :, bass.ds(col, P)])
                            v = 6 * m + off
                            if not (first and off == 0):
                                late_load(sp, v)

                late_load(sp, 1)
                mix_loads(0, first=True)
                with sp.Fori(1, C // 2) as m:
                    mix_loads(m)
                for k in range(2):
                    load_unit(sp, U_OUT + k, w_out_v[:, :, k * P:(k + 1) * P])

            @block.gpsimd
            def _(pool):
                with pool.Fori(0, C // 2) as m:
                    for r in range(2):
                        pool.wait_ge(m_ready, 2 * m + r + 1)
                        pool.dma_start(merged_dram[bass.ds(2 * m + r, 1)].rearrange("a p t -> p (a t)"),
                                       mout[r][:, :]).then_inc(m_stored[r], 16)
                for r in range(2):
                    pool.wait_ge(m_stored[r], 16 * (C // 2))

            @block.tensor
            def _(pe):
                def mix(m):
                    for r in range(2):
                        n = 2 * m + r
                        for k in range(2):
                            u = unit(U_MIX, m, 6, 3 * r + k)
                            z_unit(pe, u, U_MIX // 2 + 2 * m + r)
                            late_pe(pe, 6 * m + 3 * r + k)
                        u = unit(U_MIX, m, 6, 3 * r + 2)
                        s = slot(u)
                        pe.wait_ge(lo_ready, u + 1)
                        pe.wait_ge(mix_free, n + 1)
                        for cc in range(QC):
                            three_pass(pe, bank[2][:, :], s, cc, y_hi[:, cc, :], y_lo[:, cc, :],
                                       cc == 0, cc == QC - 1)
                        pe.wait_ge(yp_halves, PC)
                        for cc in range(PC):
                            mm = three_pass(pe, bank[3][:, :], s, QC + cc, yp_hi[:, cc, :], yp_lo[:, cc, :],
                                            cc == 0, cc == PC - 1)
                        mm.then_inc(unit_done, 1)
                        late_pe(pe, 6 * m + 3 * r + 2)

                with pe.Fori(0, C // 2) as m:
                    mix(m)

            @block.scalar
            def _(act):
                def mix(m, first=False):
                    for r in range(2):
                        n = 2 * m + r
                        for k in range(3):
                            off = 3 * r + k
                            u = unit(U_MIX, m, 6, off)
                            split_hi(act, unit(U_MIX, m, 6, off + 1), lands_in(U_MIX, m, 6, off + 1))
                            if first and off == 0:
                                for j in range(PC):
                                    act.wait_ge(yp_landed, 16 * (j + 1))
                                    act.activation(yp_hi[:, j, :], ypin[:, :], ACT.Copy).then_inc(yp_hi_done, 1)
                            if k < 2:
                                act.wait_ge(unit_done, u + 1)
                                act.wait_ge(mix_free, n + 1)
                                act.activation((sga, sgp)[k][:, :], bank[slot(u)][:, :], ACT.Sigmoid)\
                                   .then_inc(sig_ready, 1)
                                act.wait_ge(sig_ready, 2 * n + k + 1)
                                act.sem_inc(z_free[slot(u)], 1)

                mix(0, first=True)
                with act.Fori(1, C // 2) as m:
                    mix(m)

            @block.vector
            def _(dve):
                def mix(m, first=False):
                    for r in range(2):
                        n = 2 * m + r
                        for k in range(3):
                            off = 3 * r + k
                            u = unit(U_MIX, m, 6, off)
                            v = 6 * m + off
                            split_lo(dve, unit(U_MIX, m, 6, off + 1))
                            if first and off == 0:
                                for j in range(PC):
                                    dve.wait_ge(yp_hi_done, j + 1)
                                    dve.tensor_tensor(yp_lo[:, j, :], ypin[:, :], yp_hi[:, j, :].bitcast(F32),
                                                      ALU.subtract).then_inc(yp_halves, 1)
                            else:
                                late_column(dve, v - 1)
                            late_sums(dve, v)
                        u = unit(U_MIX, m, 6, 3 * r + 2)
                        dve.wait_ge(unit_done, u + 1)
                        dve.wait_ge(sig_ready, 2 * n + 2)
                        if not first:
                            dve.wait_ge(m_stored[r], 16 * m)
                        dve.tensor_tensor(mout[r][:, :], sga[:, :], bank[2][:, :], ALU.mult).then_inc(mix_step, 1)
                        dve.tensor_tensor(mtmp[:, :], sgp[:, :], bank[3][:, :], ALU.mult).then_inc(mix_step, 1)
                        dve.wait_ge(mix_step, 2 * n + 2)
                        dve.sem_inc(mix_free, 1)
                        dve.tensor_tensor(mout[r][:, :], mout[r][:, :], mtmp[:, :], ALU.add).then_inc(m_ready, 1)
                        dve.wait_ge(m_ready, n + 1)

                mix(0, first=True)
                with dve.Fori(1, C // 2) as m:
                    mix(m)
                late_column(dve, 3 * C - 1)

        mg_landed = [sem(f"mg_landed{s}") for s in range(2)]
        mg_hi = sem("mg_hi")
        mg_ready = sem("mg_ready")
        xin_landed = [sem(f"xin_landed{s}") for s in range(2)]
        x1_ready = sem("x1_ready")
        x1_kept = sem("x1_kept")
        x1_stored = [sem(f"x1_stored{s}") for s in range(2)]
        x1_sq = sem("x1_sq")
        x1_ss = sem("x1_ss")
        r2_root = sem("r2_root")
        r2_ready = sem("r2_ready")
        h2_full = sem("h2_full")
        h2_hi = sem("h2_hi")
        h2_ready = sem("h2_ready")
        sk_landed = sem("sk_landed")
        sk_tr = sem("sk_tr")
        sk_ready = sem("sk_ready")
        q_ready = sem("q_ready")
        sc_done = sem("sc_done")
        sc_ready = sem("sc_ready")
        h2_step = sem("h2_step")
        mul2_ready = sem("mul2_ready")
        Z_OUT = U_MIX // 2 + C
        down_v = expert_down[0].rearrange("(b p) d -> b p d", p=P)
        down_landed = [sem(f"down_landed{s}") for s in range(2)]

        with nc.Block() as block:
            @block.sync
            def _(sp):
                sp.dma_start(skrow[:, :, :], sub_keys[0].rearrange("h s k d -> k (h s) d")).then_inc(sk_landed, 16)
                for cc in range(C):
                    s = cc % 2
                    if cc >= 2:
                        sp.wait_ge(mg_ready, cc - 1)
                    sp.dma_start(mgin[s][:, :], merged_dram[cc]).then_inc(mg_landed[s], 16)

                def outs(m, first=False):
                    for s in range(2):
                        n = 2 * m + s
                        if not first:
                            load_unit(sp, unit(U_OUT, m, 2, s), w_out_v[:, :, bass.ds(n * P, P)])
                            sp.wait_ge(x1_ready, n - 1)
                        sp.dma_start(xtin[s][:, :], xt_dram[bass.ds(n, 1)].rearrange("a p t -> p (a t)"))\
                          .then_inc(xin_landed[s], 16)

                outs(0, first=True)
                with sp.Fori(1, C // 2) as m:
                    outs(m)

                def queries(m):
                    for s in range(2):
                        u = unit(U_QRY, m, 2, s)
                        load_unit(sp, u, w_query_v[:, :, bass.ds((2 * m + s) * P, P)])
                        late_load(sp, 3 * C + 2 * m + s)

                with sp.Fori(0, HP // 2) as m:
                    queries(m)
                for s in range(2):
                    sp.wait_ge(lo_ready, U_END - 1 + s)
                    sp.dma_start(raw[s][:, :, :], down_v[s].rearrange("p (c d) -> p c d", c=C))\
                      .then_inc(down_landed[s], 16)

            @block.tensor
            def _(pe):
                pe.wait_ge(sk_landed, 16)
                for q in range(4):
                    for r in range(4):
                        mm = pe.transpose(bank[2 + q][:, r * P:(r + 1) * P], skrow[:, 4 * q + r, :], ident[:, :])
                    mm.then_inc(sk_tr, 1)

                def outs(m, first=False):
                    for s in range(2):
                        n = 2 * m + s
                        u = unit(U_OUT, m, 2, s)
                        pe.wait_ge(lo_ready, u + 1)
                        pe.wait_ge(z_free[s], Z_OUT + m)
                        for cc in range(C):
                            if first and s == 0:
                                pe.wait_ge(mg_ready, cc + 1)
                            mm = three_pass(pe, bank[s][:, :], s, cc, act_hi[:, cc, :], act_lo[:, cc, :],
                                            cc == 0, cc == C - 1)
                        mm.then_inc(unit_done, 1)
                        if not (first and s == 0):
                            squares(n - 1, 1 - s, first and s == 1, False)

                def squares(n, s, start, stop):
                    pe.wait_ge(x1_sq, n + 1)
                    pe.matmul(B_SUM[:, :], ones[:, :], sq3[s][:, :], start=start, stop=stop,
                              skip_group_check=True).then_inc(x1_ss, 1)

                outs(0, first=True)
                with pe.Fori(1, C // 2) as m:
                    outs(m)
                squares(C - 1, 1, False, True)

                def sub_scores(m, s):
                    n = 2 * m + s
                    pe.wait_ge(q_ready, n + 1)
                    pe.wait_ge(sc_ready, n)
                    for tb in range(TB):
                        mm = pe.matmul(bank[2][:, tb * P:(tb + 1) * P], qsb[s][:, tb * P:(tb + 1) * P],
                                       skt[:, bass.ds(n, 1), :].rearrange("p a k -> p (a k)"),
                                       start=True, stop=True)
                    mm.then_inc(sc_done, 1)

                def queries(m, first=False):
                    for s in range(2):
                        u = unit(U_QRY, m, 2, s)
                        pe.wait_ge(lo_ready, u + 1)
                        pe.wait_ge(z_free[s], Z_OUT + C // 2 + m)
                        for cc in range(C):
                            if first and s == 0:
                                pe.wait_ge(h2_ready, cc + 1)
                            mm = three_pass(pe, bank[s][:, :], s, cc, act_hi[:, cc, :], act_lo[:, cc, :],
                                            cc == 0, cc == C - 1)
                        mm.then_inc(unit_done, 1)
                        late_pe(pe, 3 * C + 2 * m + s)
                        if first and s == 0:
                            pe.wait_ge(sk_ready, 4)
                        else:
                            sub_scores(m if s else m - 1, 1 - s)

                queries(0, first=True)
                with pe.Fori(1, HP // 2) as m:
                    queries(m)
                sub_scores(HP // 2 - 1, 1)

            @block.scalar
            def _(act):
                for q in range(4):
                    act.wait_ge(sk_tr, q + 1)
                    act.activation(skt[:, 4 * q:4 * q + 4, :], bank[2 + q][:, :].rearrange("p (r k) -> p r k", r=4),
                                   ACT.Copy).then_inc(sk_ready, 1)
                for cc in range(C):
                    s = cc % 2
                    act.wait_ge(mg_landed[s], 16 * (cc // 2 + 1))
                    act.activation(act_hi[:, cc, :], mgin[s][:, :], ACT.Copy).then_inc(mg_hi, 1)

                def outs(m, first=False):
                    for s in range(2):
                        n = 2 * m + s
                        split_hi(act, unit(U_OUT, m, 2, s + 1), lands_in(U_OUT, m, 2, s + 1))
                        act.wait_ge(x1_ready, n + 1)
                        if not first:
                            act.wait_ge(x1_ss, n - 1)
                        act.activation(sq3[s][:, :], x1c[s][:, :], ACT.Square).then_inc(x1_sq, 1)

                outs(0, first=True)
                with act.Fori(1, C // 2) as m:
                    outs(m)
                act.wait_ge(x1_ss, C)
                act.activation(rstd2[:, :], B_SUM[:, :], ACT.Sqrt, bias=eps[:, :], scale=1.0 / D)\
                   .then_inc(r2_root, 1)
                for cc in range(C):
                    act.wait_ge(h2_full, cc + 1)
                    act.activation(act_hi[:, cc, :], h2full[cc % 2][:, :], ACT.Copy).then_inc(h2_hi, 1)

                def queries(m, first=False, last=False):
                    for s in range(2):
                        n = 2 * m + s
                        u = unit(U_QRY, m, 2, s)
                        if not (last and s == 1):
                            split_hi(act, unit(U_QRY, m, 2, s + 1), lands_in(U_QRY, m, 2, s + 1))
                        act.wait_ge(unit_done, u + 1)
                        if not first:
                            act.wait_ge(sc_done, n - 1)
                        act.activation(qsb[s][:, :], bank[s][:, :], ACT.Copy).then_inc(q_ready, 1)
                        act.wait_ge(q_ready, n + 1)
                        act.sem_inc(z_free[s], 1)

                queries(0, first=True)
                with act.Fori(1, HP // 2 - 1) as m:
                    queries(m)
                queries(HP // 2 - 1, last=True)

            @block.vector
            def _(dve):
                for cc in range(C):
                    s = cc % 2
                    dve.wait_ge(mg_hi, cc + 1)
                    dve.tensor_tensor(act_lo[:, cc, :], mgin[s][:, :], act_hi[:, cc, :].bitcast(F32),
                                      ALU.subtract).then_inc(mg_ready, 1)

                def outs(m, first=False):
                    for s in range(2):
                        n = 2 * m + s
                        u = unit(U_OUT, m, 2, s)
                        split_lo(dve, unit(U_OUT, m, 2, s + 1))
                        if not first:
                            dve.wait_ge(x1_stored[s], 16 * m)
                            dve.wait_ge(x1_sq, n - 1)
                            dve.wait_ge(x1_kept, n - 1)
                        dve.wait_ge(unit_done, u + 1)
                        dve.wait_ge(xin_landed[s], 16 * m + 16)
                        dve.scalar_tensor_tensor(out=x1c[s][:, :], in0=bank[s][:, :],
                                                 scalar=mod[:, bass.ds(2 * C + n, 1)], in1=xtin[s][:, :],
                                                 op0=ALU.mult, op1=ALU.add).then_inc(x1_ready, 1)
                        dve.wait_ge(x1_ready, n + 1)
                        dve.sem_inc(z_free[s], 1)

                outs(0, first=True)
                with dve.Fori(1, C // 2) as m:
                    outs(m)
                dve.scalar_tensor_tensor(out=mul2[:, :], in0=mod[:, 4 * C:5 * C], scalar=1.0,
                                         in1=vec_b[:, 0:C], op0=ALU.add, op1=ALU.mult).then_inc(mul2_ready, 1)
                dve.wait_ge(r2_root, 1)
                dve.reciprocal(rstd2[:, :], rstd2[:, :]).then_inc(r2_ready, 1)
                dve.wait_ge(r2_ready, 1)
                dve.wait_ge(mul2_ready, 1)
                dve.wait_ge(x1_kept, C)
                dve.wait_ge(unit_done, U_QRY)
                for cc in range(C):
                    if cc >= 2:
                        dve.wait_ge(h2_ready, cc - 1)
                    dve.tensor_tensor(h2full[cc % 2][:, :], x1t[:, cc, :], rstd2[:, :], ALU.mult)\
                       .then_inc(h2_step, 1)
                    dve.wait_ge(h2_step, cc + 1)
                    dve.tensor_scalar(h2full[cc % 2][:, :], h2full[cc % 2][:, :], mul2[:, cc:cc + 1],
                                      mod[:, 3 * C + cc:3 * C + cc + 1], ALU.mult, ALU.add).then_inc(h2_full, 1)
                    dve.wait_ge(h2_hi, cc + 1)
                    dve.tensor_tensor(act_lo[:, cc, :], h2full[cc % 2][:, :], act_hi[:, cc, :].bitcast(F32),
                                      ALU.subtract).then_inc(h2_ready, 1)

                def take_scores(m, s):
                    n = 2 * m + s
                    dve.wait_ge(sc_done, n + 1)
                    dve.tensor_scalar(s_all[:, :, bass.ds(n, 1), :].rearrange("p b a k -> p b (a k)"),
                                      bank[2][:, :].rearrange("p (b k) -> p b k", b=TB), 1.0, None,
                                      ALU.mult).then_inc(sc_ready, 1)

                def queries(m, first=False, last=False):
                    for s in range(2):
                        v = 3 * C + 2 * m + s
                        if not (last and s == 1):
                            split_lo(dve, unit(U_QRY, m, 2, s + 1))
                        if not (first and s == 0):
                            late_column(dve, v - 1)
                        late_sums(dve, v)
                        if not (first and s == 0):
                            take_scores(m if s else m - 1, 1 - s)

                dve.wait_ge(sk_ready, 4)
                for s in range(2):
                    dve.wait_ge(x1_stored[s], 16 * (C // 2))
                queries(0, first=True)
                with dve.Fori(1, HP // 2 - 1) as m:
                    queries(m)
                queries(HP // 2 - 1, last=True)
                take_scores(HP // 2 - 1, 1)
                late_column(dve, 4 * C - 1)

            @block.gpsimd
            def _(pool):
                def keep(m):
                    for s in range(2):
                        n = 2 * m + s
                        pool.wait_ge(x1_ready, n + 1)
                        pool.dma_start(x1_dram[bass.ds(n, 1)].rearrange("a p t -> p (a t)"), x1c[s][:, :])\
                            .then_inc(x1_stored[s], 16)
                        pool.tensor_copy(x1t[:, bass.ds(n, 1), :].rearrange("p a t -> p (a t)"), x1c[s][:, :])\
                            .then_inc(x1_kept, 1)

                with pool.Fori(0, C // 2) as m:
                    keep(m)
                for s in range(2):
                    pool.wait_ge(x1_stored[s], 16 * (C // 2))

        dtr_done = sem("dtr_done")
        d_hi = sem("d_hi")
        d_lo = sem("d_lo")
        a_done = sem("a_done")
        a_ready = sem("a_ready")
        tk = sem("tk")
        tk_seen = sem("tk_seen")
        sm_step = sem("sm_step")
        sm_exp = sem("sm_exp")
        rt_done = sem("rt_done")
        rt_ready = sem("rt_ready")
        oh_ready = sem("oh_ready")
        oh_step = sem("oh_step")
        g_copied = sem("g_copied")
        QB = 4 * P
        NT = TB * PH
        G_PER = 8
        NGB = T // G_PER
        E1, E2 = NT, NT + NGB
        assert E2 <= EB - 1 and GT % (2 * G_PER) == 0

        with nc.Block() as block:
            @block.sync
            def _(sp):
                def step(i, s, last=False):
                    if not last:
                        sp.wait_ge(dtr_done, 4 * i + 4)
                        sp.dma_start(raw[s][:, :, :],
                                     down_v[bass.ds(i + 2, 1)].rearrange("a p (c d) -> p (a c) d", c=C))\
                          .then_inc(down_landed[s], 16)
                    sp.wait_ge(a_ready, i + 1)
                    sp.dma_start(act_dram[bass.ds(i, 1)].rearrange("a p t -> p (a t)"), aout[s][:, :])\
                      .then_inc(a_stored[s], 16)

                with sp.Fori(0, EB // 2 - 1) as m:
                    step(2 * m, 0)
                    step(2 * m + 1, 1)
                step(EB - 2, 0, last=True)
                step(EB - 1, 1, last=True)
                for s in range(2):
                    sp.wait_ge(a_stored[s], 16 * (EB // 2) + 16)

            @block.gpsimd
            def _(pool):
                for b in range(T // GT):
                    s = b % 2
                    pool.wait_ge(g_copied, (b + 1) * GT // 4)
                    for k in range(2):
                        eb = slice(k * EB // 2, (k + 1) * EB // 2)
                        pool.dma_start(gate_dram[eb, :, b * GT:(b + 1) * GT].rearrange("i j t -> j i t"),
                                       gbuf[s][:, eb, :]).then_inc(g_stored[s], 16)
                for s in range(2):
                    pool.wait_ge(g_stored[s], 32 * (T // GT // 2))

            @block.tensor
            def _(pe):
                def quarter_in(i, s, q):
                    for r in range(4):
                        mm = pe.transpose(bank[q][:, r * P:(r + 1) * P], raw[s][:, 4 * q + r, :], ident[:, :])
                    mm.then_inc(dtr_done, 1)

                def block_products(i, s, following=True, extra=None):
                    if following:
                        pe.wait_ge(down_landed[1 - s], 16 * ((i + 1) // 2 if isinstance(i, int) else half_of(i, s)) + 16)
                    for q in range(4):
                        pe.wait_ge(d_lo, 4 * i + q + 1)
                        if following:
                            quarter_in(i + 1, 1 - s, q)
                        if q == 0:
                            pe.wait_ge(a_ready, i - 1 if not isinstance(i, int) else max(i - 1, 0))
                        for r in range(4):
                            cc = 4 * q + r
                            mm = three_pass(pe, bank[4 + s][:, :], s, cc, act_hi[:, cc, :], act_lo[:, cc, :],
                                            cc == 0, cc == C - 1)
                        if q == 3:
                            mm.then_inc(a_done, 1)
                        if extra and q % 2:
                            extra(q // 2)

                def half_of(i, s):
                    return halves[id(i)][1]

                halves = {}

                def pair(m, i0, extra=None, last=False):
                    for s in range(2):
                        i = i0 + 2 * m + s
                        if not isinstance(i, int):
                            halves[id(i)] = (i, i0 // 2 + m + s)
                        block_products(i, s, following=not (last and s == 1),
                                       extra=(lambda k, s=s: extra(m, s, k)) if extra else None)

                pe.wait_ge(down_landed[0], 16)
                for q in range(4):
                    quarter_in(0, 0, q)
                pair(0, 0)
                with pe.Fori(1, E1 // 2) as m:
                    pair(m, 0)
                for k, src in enumerate((top_all, i_all, j_all)):
                    pe.wait_ge(sm_step, 4)
                    if k:
                        pe.wait_ge(rt_ready, k)
                    for tb in range(TB):
                        mm = pe.transpose(bank[6][:, tb * P:(tb + 1) * P], src[:, tb, :], ident[:, :])
                    mm.then_inc(rt_done, 1)
                pe.wait_ge(rt_ready, 3)

                def gates(m, s, k):
                    n = 2 * (2 * m + s) + k
                    pe.wait_ge(oh_ready, n + 1)
                    pe.wait_ge(g_copied, n - 1 if not isinstance(n, int) else max(n - 1, 0))
                    for t in range(4):
                        mm = pe.matmul(bank[6 + k][:, t * P:(t + 1) * P], oh_j[:, t, :], oh_i[:, t, :],
                                       start=True, stop=True)
                    mm.then_inc(g_done, 1)

                pair(0, E1, extra=gates)
                with pe.Fori(1, NGB // 2) as m:
                    pair(m, E1, extra=gates)
                with pe.Fori(0, (EB - E2) // 2 - 1) as m:
                    pair(m, E2)
                pair(EB // 2 - 1, 0, last=True)

            @block.scalar
            def _(act):
                def highs(i, s):
                    for q in range(4):
                        act.wait_ge(dtr_done, 4 * i + q + 1)
                        act.activation(w_hi_t[s][:, 4 * q:4 * q + 4, :],
                                       bank[q][:, :].rearrange("p (r e) -> p r e", r=4), ACT.Copy)\
                           .then_inc(d_hi, 1)

                def gelu(i, s, m):
                    act.wait_ge(a_done, i + 1)
                    act.wait_ge(a_stored[s], 16 * m + 16)
                    act.activation(aout[s][:, :], bank[4 + s][:, :], ACT.Gelu).then_inc(a_ready, 1)

                highs(0, 0)
                with act.Fori(0, E1 // 2) as m:
                    for s in range(2):
                        highs(2 * m + s + 1, 1 - s)
                        gelu(2 * m + s, s, m)
                act.wait_ge(sm_step, 1)
                act.activation(top_all[:, :, :], top_all[:, :, :], ACT.Exp).then_inc(sm_exp, 1)
                for k, dst in enumerate((gate_t, i_t, j_t)):
                    act.wait_ge(rt_done, k + 1)
                    act.activation(dst[:, :], bank[6][:, :], ACT.Copy).then_inc(rt_ready, 1)
                rounds = GT // G_PER

                def two_stored_blocks(b, first=False):
                    for gs in range(2):
                        if not first:
                            act.wait_ge(g_stored[gs], 32 * b)
                        for j in range(rounds // 2):
                            for s in range(2):
                                w = gs * rounds + 2 * j + s
                                i = E1 + 2 * rounds * b + w
                                n = 2 * (2 * rounds * b + w)
                                highs(i + 1, 1 - s)
                                for k in range(2):
                                    act.wait_ge(g_done, n + k + 2)
                                    off = (2 * j + s) * G_PER + 4 * k
                                    act.activation(gbuf[gs][:, :, off:off + 4].rearrange("p i t -> p t i"),
                                                   bank[6 + k][:, :].rearrange("p (t i) -> p t i", t=4),
                                                   ACT.Copy).then_inc(g_copied, 1)
                                gelu(i, s, E1 // 2 + rounds * b + w // 2)

                two_stored_blocks(0, first=True)
                with act.Fori(1, T // GT // 2) as b:
                    two_stored_blocks(b)
                with act.Fori(E2 // 2, EB // 2 - 1) as m:
                    for s in range(2):
                        highs(2 * m + s + 1, 1 - s)
                        gelu(2 * m + s, s, m)
                highs(EB - 1, 1)
                gelu(EB - 2, 0, EB // 2 - 1)
                gelu(EB - 1, 1, EB // 2 - 1)

            @block.vector
            def _(dve):
                def low(i, s, q):
                    dve.wait_ge(d_hi, 4 * i + q + 1)
                    dve.tensor_tensor(w_lo_t[s][:, 4 * q:4 * q + 4, :],
                                      bank[q][:, :].rearrange("p (r e) -> p r e", r=4),
                                      w_hi_t[s][:, 4 * q:4 * q + 4, :].bitcast(F32), ALU.subtract)\
                       .then_inc(d_lo, 1)

                STEPS = 19
                BEFORE_MAX = (1, 2, 3, 4, 5, 6, 7, 8, 10, 11, 12, 13)

                def step(v, k, ins):
                    ins.then_inc(tk, 1)
                    dve.wait_ge(tk, STEPS * v + k)
                    if k in BEFORE_MAX:
                        dve.sem_inc(tk_seen, 1)

                def top_keys(v, tb, h2, p):
                    k = 1 + 4 * p
                    if p == 0:
                        step(v, 1, dve.tensor_scalar(srow[:, :, :], s_all[:, tb, bass.ds(h2, 2), :], 1.0, None,
                                                     ALU.mult))
                    step(v, k + 1, dve.max(val[:, p, 0:8], srow[:, p, :]))
                    dve.max_index(idx[:, p, 0:8], val[:, p, 0:8], srow[:, p, :])
                    step(v, k + 2, dve.match_replace(srow2[:, p, :], val[:, p, 0:8], srow[:, p, :], NEG))
                    step(v, k + 3, dve.max(val[:, p, 8:16], srow2[:, p, :]))
                    step(v, k + 4, dve.max_index(idx[:, p, 8:16], val[:, p, 8:16], srow2[:, p, :]))

                def top_sums(v):
                    step(v, 10, dve.tensor_tensor(
                        cand[:, :, :], val[:, 0, :].unsqueeze(2).to_broadcast([P, TOPK, TOPK]),
                        val[:, 1, :].unsqueeze(1).to_broadcast([P, TOPK, TOPK]), ALU.add))
                    flat, flat2 = (t[:, :, :].rearrange("p a b -> p (a b)") for t in (cand, cand2))
                    step(v, 11, dve.max(topv[:, 0:8], flat))
                    dve.max_index(pos[:, 0:8], topv[:, 0:8], flat)
                    step(v, 12, dve.match_replace(flat2, topv[:, 0:8], flat, NEG))
                    step(v, 13, dve.max(topv[:, 8:16], flat2))
                    step(v, 14, dve.max_index(pos[:, 8:16], topv[:, 8:16], flat2))

                def indices(v, tb, h2):
                    dve.tensor_scalar(posab[:, 0, :], pos[:, :], 4, None, ALU.logical_shift_right)
                    step(v, 15, dve.tensor_scalar(posab[:, 1, :], pos[:, :], TOPK - 1, None, ALU.bitwise_and))
                    dve.tensor_copy(posf[:, :, :], posab[:, :, :])
                    step(v, 16, dve.tensor_copy(idxf[:, :, :], idx[:, :, :]))
                    step(v, 17, dve.tensor_tensor(
                        pick[:, :, :, :].rearrange("p a k m -> p (a k) m"),
                        posf[:, :, :].rearrange("p a k -> p (a k)").unsqueeze(2).to_broadcast([P, 2 * TOPK, TOPK]),
                        iota_keys[:, 0:TOPK].unsqueeze(1).to_broadcast([P, 2 * TOPK, TOPK]), ALU.is_equal))
                    step(v, 18, dve.tensor_tensor(
                        pick2[:, :, :, :], pick[:, :, :, :],
                        idxf[:, :, :].unsqueeze(2).to_broadcast([P, 2, TOPK, TOPK]), ALU.mult))
                    hk = bass.ds(h2 * (TOPK // 2), TOPK)
                    dve.tensor_reduce(i_all[:, tb, hk], pick2[:, 0, :, :], AX.X, ALU.add)
                    dve.tensor_reduce(j_all[:, tb, hk], pick2[:, 1, :, :], AX.X, ALU.add)
                    step(v, 19, dve.tensor_scalar(top_all[:, tb, hk], topv[:, :], topv[:, 0:1], None,
                                                  ALU.subtract))

                for q in range(4):
                    low(0, 0, q)
                for tb in range(TB):
                    with dve.Fori(0, PH // 2) as m:
                        for s in range(2):
                            v = tb * PH + 2 * m + s
                            h2 = 4 * m + 2 * s
                            low(v + 1, 1 - s, 0)
                            top_keys(v, tb, h2, 0)
                            low(v + 1, 1 - s, 1)
                            top_keys(v, tb, h2, 1)
                            low(v + 1, 1 - s, 2)
                            top_sums(v)
                            low(v + 1, 1 - s, 3)
                            indices(v, tb, h2)
                dve.sem_inc(sm_step, 1)
                dve.wait_ge(sm_exp, 1)
                heads = top_all[:, :, :].rearrange("p b (h k) -> p (b h) k", k=TOPK)
                dve.tensor_reduce(zsum[:, :], heads, AX.X, ALU.add).then_inc(sm_step, 1)
                dve.wait_ge(sm_step, 2)
                dve.reciprocal(zsum[:, :], zsum[:, :]).then_inc(sm_step, 1)
                dve.wait_ge(sm_step, 3)
                dve.tensor_tensor(heads, heads, zsum[:, :].unsqueeze(2).to_broadcast([P, TB * PH, TOPK]),
                                  ALU.mult).then_inc(sm_step, 1)
                dve.wait_ge(rt_ready, 3)

                def one_hots(n):
                    t = bass.ds(4 * n, 4)
                    dve.wait_ge(g_done, n + 1)
                    keys = iota_keys[:, :].unsqueeze(1).to_broadcast([P, 4, P])
                    dve.tensor_tensor(oh_j[:, :, :], j_t[:, t].unsqueeze(2).to_broadcast([P, 4, P]), keys,
                                      ALU.is_equal).then_inc(oh_step, 1)
                    dve.tensor_tensor(oh_i[:, :, :], i_t[:, t].unsqueeze(2).to_broadcast([P, 4, P]), keys,
                                      ALU.is_equal).then_inc(oh_step, 1)
                    dve.wait_ge(oh_step, 2 * n + 2)
                    dve.tensor_tensor(oh_i[:, :, :], oh_i[:, :, :],
                                      gate_t[:, t].unsqueeze(2).to_broadcast([P, 4, P]), ALU.mult)\
                       .then_inc(oh_ready, 1)

                with dve.Fori(0, NGB // 2) as m:
                    for s in range(2):
                        for q in range(4):
                            if q % 2 == 0:
                                one_hots(4 * m + 2 * s + q // 2)
                            low(E1 + 2 * m + s + 1, 1 - s, q)
                with dve.Fori(E2 // 2, EB // 2 - 1) as m:
                    for s in range(2):
                        for q in range(4):
                            low(2 * m + s + 1, 1 - s, q)
                for q in range(4):
                    low(EB - 1, 1, q)

        up_v = expert_up[0].rearrange("(b p) (h d) -> h b p d", p=P, h=2)
        up_landed = [sem(f"up_landed{s}") for s in range(2)]
        ag_landed = [sem(f"ag_landed{s}") for s in range(2)]
        up_hi_done = sem("up_hi_done")
        up_ready = sem("up_ready")
        ag_full = sem("ag_full")
        ag_hi_done = sem("ag_hi_done")
        ag_ready = sem("ag_ready")
        f_done = sem("f_done")
        x1f_landed = sem("x1f_landed")
        half_read = sem("half_read")
        otr_done = sem("otr_done")
        o_copied = sem("o_copied")
        out_stored = sem("out_stored")

        with nc.Block() as block:
            @block.sync
            def _(sp):
                sp.dma_start(x1f[:, :, :], x1_dram.rearrange("c p t -> p c t")).then_inc(x1f_landed, 16)

                def load(h, i, s, k, first=False):
                    n = h * EB + i
                    if not first:
                        sp.wait_ge(up_ready, n - 1)
                        sp.wait_ge(ag_full, n - 1)
                    sp.dma_start(up_raw[s][:, :], up_v[h, bass.ds(i, 1)].rearrange("a p d -> p (a d)"))\
                      .then_inc(up_landed[s], 16)
                    sp.dma_start(a_in[s][:, :], act_dram[bass.ds(i, 1)].rearrange("a p t -> p (a t)"))\
                      .then_inc(ag_landed[s], 16)
                    sp.dma_start(g_in[s][:, :], gate_dram[bass.ds(i, 1)].rearrange("a p t -> p (a t)"))\
                      .then_inc(ag_landed[s], 16)

                for h in range(2):
                    if h == 0:
                        load(0, 0, 0, 0, first=True)
                        load(0, 1, 1, 0, first=True)
                    with sp.Fori(1 if h == 0 else 0, EB // 2) as m:
                        for s in range(2):
                            load(h, 2 * m + s, s, m)
                for tb in range(TB):
                    sp.wait_ge(o_copied, 4 * (tb + 1))
                    sp.dma_start(out_v[tb * P:(tb + 1) * P, :], orow[tb][:, :]).then_inc(out_stored, 16)
                sp.wait_ge(out_stored, 16 * TB)

            @block.tensor
            def _(pe):
                def experts(h, i, s, start, stop):
                    n = h * EB + i
                    pe.wait_ge(up_ready, n + 1)
                    pe.wait_ge(ag_ready, n + 1)
                    for dc in range(HC):
                        cols = slice(dc * P, (dc + 1) * P)
                        pe.matmul(bank[dc][:, :], up_hi[s][:, cols], ag_hi[s][:, :], start=start, stop=False,
                                  skip_group_check=True)
                        pe.matmul(bank[dc][:, :], up_hi[s][:, cols], ag_lo[s][:, :], start=False, stop=False,
                                  skip_group_check=True)
                        mm = pe.matmul(bank[dc][:, :], up_lo[s][:, cols], ag_hi[s][:, :], start=False,
                                       stop=stop, skip_group_check=True)
                    mm.then_inc(f_done, 1)

                for h in range(2):
                    if h:
                        pe.wait_ge(half_read, HC)
                    experts(h, 0, 0, True, False)
                    experts(h, 1, 1, False, False)
                    with pe.Fori(1, EB // 2 - 1) as m:
                        experts(h, 2 * m, 0, False, False)
                        experts(h, 2 * m + 1, 1, False, False)
                    experts(h, EB - 2, 0, False, False)
                    experts(h, EB - 1, 1, False, True)
                pe.wait_ge(half_read, 2 * HC)
                for tb in range(TB):
                    for q in range(4):
                        n = 4 * tb + q
                        if n >= 8:
                            pe.wait_ge(o_copied, n - 7)
                        for r in range(4):
                            mm = pe.transpose(bank[n % 8][:, r * P:(r + 1) * P],
                                              x1f[:, 4 * q + r, tb * P:(tb + 1) * P], ident[:, :])
                        mm.then_inc(otr_done, 1)

            @block.scalar
            def _(act):
                def halves(h, i, s, m, first=False):
                    n = h * EB + i
                    act.wait_ge(up_landed[s], 16 * (h * (EB // 2) + m + 1))
                    if not first:
                        act.wait_ge(f_done, n - 1)
                    act.activation(up_hi[s][:, :], up_raw[s][:, :], ACT.Copy).then_inc(up_hi_done, 1)
                    act.wait_ge(ag_full, n + 1)
                    act.activation(ag_hi[s][:, :], ag[s][:, :], ACT.Copy).then_inc(ag_hi_done, 1)

                halves(0, 0, 0, 0, first=True)
                halves(0, 1, 1, 0, first=True)
                for h in range(2):
                    with act.Fori(1 if h == 0 else 0, EB // 2) as m:
                        halves(h, 2 * m, 0, m)
                        halves(h, 2 * m + 1, 1, m)

            @block.vector
            def _(dve):
                def halves(h, i, s, m, first=False):
                    n = h * EB + i
                    if not first:
                        dve.wait_ge(f_done, n - 1)
                    dve.wait_ge(ag_landed[s], 32 * (h * (EB // 2) + m + 1))
                    if not first:
                        dve.wait_ge(ag_ready, n - 1)
                    dve.tensor_tensor(ag[s][:, :], a_in[s][:, :], g_in[s][:, :], ALU.mult).then_inc(ag_full, 1)
                    dve.wait_ge(up_hi_done, n + 1)
                    dve.tensor_tensor(up_lo[s][:, :], up_raw[s][:, :], up_hi[s][:, :].bitcast(F32),
                                      ALU.subtract).then_inc(up_ready, 1)
                    dve.wait_ge(ag_hi_done, n + 1)
                    dve.tensor_tensor(ag_lo[s][:, :], ag[s][:, :], ag_hi[s][:, :].bitcast(F32),
                                      ALU.subtract).then_inc(ag_ready, 1)

                halves(0, 0, 0, 0, first=True)
                halves(0, 1, 1, 0, first=True)
                for h in range(2):
                    with dve.Fori(1 if h == 0 else 0, EB // 2) as m:
                        halves(h, 2 * m, 0, m)
                        halves(h, 2 * m + 1, 1, m)
                    if h == 0:
                        dve.wait_ge(x1f_landed, 16)
                    dve.wait_ge(f_done, (h + 1) * EB)
                    for dc in range(HC):
                        n = h * HC + dc
                        dve.scalar_tensor_tensor(out=x1f[:, n, :], in0=bank[dc][:, :],
                                                 scalar=mod[:, 5 * C + n:5 * C + n + 1], in1=x1f[:, n, :],
                                                 op0=ALU.mult, op1=ALU.add).then_inc(half_read, 1)
                for tb in range(TB):
                    for q in range(4):
                        n = 4 * tb + q
                        dve.wait_ge(otr_done, n + 1)
                        dve.tensor_copy(orow[tb][:, 4 * q * P:(4 * q + 4) * P], bank[n % 8][:, :])\
                           .then_inc(o_copied, 1)


_INS = ['x', 'c', 'w_ada', 'b_ada', 'norm1_g', 'w_in', 'q_norm_g', 'k_norm_g', 'attn_sinks', 'pool_group_w',
        'pool_scale', 'w_branch_attn', 'w_branch_pool', 'w_out', 'norm2_g', 'w_query', 'sub_keys',
        'expert_down', 'expert_up']


def kernel(**inputs):
    import numpy as _np
    import concourse.bacc as _bacc
    from concourse import mybir as _mybir
    from concourse.bass_utils import run_bass_kernel_spmd as _run

    nc = _bacc.Bacc("TRN2", target_bir_lowering=False, num_devices=1)
    arrays, args = {}, []
    for name in _INS:
        a = _np.ascontiguousarray(inputs[name])
        arrays[f"in_{name}"] = a
        args.append(nc.dram_tensor(f"in_{name}", a.shape, _mybir.dt.from_np(a.dtype), kind="ExternalInput").ap())
    args.append(nc.dram_tensor("out_x", inputs["x"].shape, _mybir.dt.float32, kind="ExternalOutput").ap())
    build(nc, *args)
    r = _run(nc, [arrays], core_ids=[0])
    return r.results[0]["out_x"]
```

```python
from contextlib import ExitStack

import concourse.bass as bass
from concourse import mybir

F32 = mybir.dt.float32
F32R = mybir.dt.float32r
U32 = mybir.dt.uint32
ALU = mybir.AluOpType
ACT = mybir.ActivationFunctionType
AX = mybir.AxisListType

P = 128


def build(nc, x, c, w_ada, b_ada, norm1_g, w_in, q_norm_g, k_norm_g, attn_sinks, pool_group_w,
          pool_scale, w_branch_attn, w_branch_pool, w_out, norm2_g, w_query, sub_keys,
          expert_down, expert_up, out):
    _, T, D = x.shape
    C = D // P
    TB = T // P
    HD = q_norm_g.shape[1]
    NQ = attn_sinks.shape[1]
    CHUNK = 64
    AW = w_branch_attn.shape[1]
    PW = w_branch_pool.shape[1]
    QC, PC = AW // P, PW // P
    NG, PG = pool_group_w.shape[1], pool_group_w.shape[2]
    WINDOWS = tuple(2 << g for g in range(NG))
    PH, NK = sub_keys.shape[1], sub_keys.shape[3]
    HP = 2 * PH
    TOPK = 16
    E = expert_down.shape[1]
    EB = E // P
    NKV = (w_in.shape[2] - AW - PW - 2 * D) // 2 // HD
    EPS = 1e-6
    SCALE = float(HD) ** -0.5
    NEG = -3.0e38
    assert C == 16 and TB == 4 and HD == 64 and NQ == 16 and NKV == 2 and NK == P and PG == 2 * P
    assert E == NK * NK and PC == C // 2 and QC == C // 2 and NG == TB

    U_K, U_V, U_Q = 0, 1, 2
    U_POOL = U_Q + QC
    U_MIX = U_POOL + PC
    U_OUT = U_MIX + 3 * C
    U_QRY = U_OUT + C
    U_END = U_QRY + HP

    NORMS = (U_K, *range(U_Q, U_POOL))

    def col_of(u):
        if u >= U_POOL:
            return AW + 2 * NKV * HD + (u - U_POOL) * P
        return (u - U_Q) * P if u >= U_Q else AW + u * P

    xt_dram = nc.dram_tensor("xt_scratch", [C, P, T], F32).ap()
    merged_dram = nc.dram_tensor("merged_scratch", [C, P, T], F32).ap()
    ypool_dram = nc.dram_tensor("ypool_scratch", [PC, P, T], F32).ap()
    x1_dram = nc.dram_tensor("x1_scratch", [C, P, T], F32).ap()
    act_dram = nc.dram_tensor("act_scratch", [EB, P, T], F32).ap()
    gate_dram = nc.dram_tensor("gate_scratch", [EB, P, T], F32).ap()

    def chunked(w):
        return w.rearrange("(c p) n -> p c n", p=P)

    w_ada_v, w_in_v, w_out_v, w_query_v = (chunked(w[0]) for w in (w_ada, w_in, w_out, w_query))
    wba_v, wbp_v = chunked(w_branch_attn[0]), chunked(w_branch_pool[0])
    out_v = out[0]

    ctx = ExitStack()
    with ctx:
        def sem(name):
            return ctx.enter_context(nc.semaphore(name))

        BASE = 16512
        KB = 1024
        END = 229368

        def at(name, shape, dt, off):
            size = 4
            for n in shape[1:]:
                size *= n
            assert BASE + off + size <= END, (name, off, size)
            return nc.alloc_sbuf_tensor_at(name, shape, dt, offset=BASE + off)

        cur = [0]

        def const(name, shape, dt=F32):
            t = at(name, shape, dt, cur[0])
            size = 4
            for n in shape[1:]:
                size *= n
            cur[0] += (size + 31) // 32 * 32
            return t

        ident = const("ident", [P, P])
        ones = const("ones", [P, P])
        blockones = const("blockones", [P, P])
        iota_keys = const("iota_keys", [P, P])
        vec_a = const("vec_a", [P, P])
        vec_b = const("vec_b", [P, 32])
        cond = const("cond", [P, C])
        mod = const("mod", [P, 6 * C])
        mul1 = const("mul1", [P, C])
        mul2 = const("mul2", [P, C])
        eps = const("eps", [P, 1])
        sinks = const("sinks", [P, NQ])
        rcount = const("rcount", [P, NG, 16])
        assert cur[0] <= 4 * KB

        o = 6 * KB
        raw = [at(f"raw{s}", [P, C, P], F32, o + 8 * KB * s) for s in range(2)]
        w_hi_t = [at(f"w_hi{s}", [P, C, P], F32R, o + 8 * KB * (2 + s)) for s in range(2)]
        w_lo_t = [at(f"w_lo{s}", [P, C, P], F32R, o + 8 * KB * (4 + s)) for s in range(2)]
        A0 = o + 48 * KB
        act_hi = at("act_hi", [P, C, T], F32R, A0)
        act_lo = at("act_lo", [P, C, T], F32R, A0 + 32 * KB)
        L0 = A0 + 64 * KB

        MOD_W = 2 * P
        mraw = [at(f"mraw{s}", [P, C, MOD_W], F32, off)
                for s, off in enumerate((A0, A0 + 16 * KB, o + 16 * KB, o + 32 * KB))]
        xt = at("xt", [P, C, T], F32, L0)
        xrow = [at(f"xrow{s}", [P, D], F32, L0 + 32 * KB + 8 * KB * s) for s in range(TB)]
        sq = [at(f"sq{s}", [P, T], F32, L0 + 64 * KB + 2 * KB * s) for s in range(2)]
        rstd = at("rstd", [P, T], F32, L0 + 68 * KB)
        hfull = [at(f"hfull{s}", [P, T], F32, L0 + 80 * KB + 2 * KB * s) for s in range(2)]
        macc_e = [at(f"macc_e{s}", [P, 2, MOD_W], F32, L0 + 70 * KB + 2 * KB * s) for s in range(2)]
        vrow_a = at("vrow_a", [P, P], F32, L0 + 74 * KB)
        vrow_b = at("vrow_b", [P, P], F32, L0 + 74 * KB + 512)
        sinkrow = at("sinkrow", [P, NQ], F32, L0 + 75 * KB)
        csig = at("csig", [P, C], F32, L0 + 75 * KB + 64)

        xn = at("xn", [P, C, T], F32, A0 + 32 * KB)
        macc = at("macc", [P, 2, 2, P], F32, L0 + 84 * KB)

        B0 = L0 + 32 * KB
        kt = at("kt", [P, T], F32, L0 + 64 * KB)
        kdup = [at(f"kdup{k}", [P, T], F32, L0 + 66 * KB + 2 * KB * k) for k in range(NKV)]
        vt = at("vt", [P, T], F32, L0 + 70 * KB)
        vrows = at("vrows", [P, TB, P], F32, L0 + 72 * KB)
        sq2 = [at(f"sqb{s}", [P, T], F32, L0 + 74 * KB + 2 * KB * s) for s in range(2)]
        rq = [at(f"rq{s}", [P, T], F32, L0 + 78 * KB + 2 * KB * s) for s in range(2)]
        qt = at("qt", [P, QC, T], F32, B0)
        y_hi = at("y_hi", [P, QC, T], F32R, B0)
        y_lo = at("y_lo", [P, QC, T], F32R, L0)
        sprob = at("sprob", [P, 4, 2 * P], F32, L0 + 16 * KB)
        prob = [at(f"prob{s}", [P, 4, 2 * P], F32, L0 + (20, 84)[s] * KB) for s in range(2)]
        prob_t = at("prob_t", [P, 4, 2, P], F32, L0 + 24 * KB)
        stat = at("stat", [P, 6, 4], F32, L0 + 28 * KB)
        PAD = 16
        pin = at("pin", [P, PAD + T], F32, L0 + 48 * KB)
        pwin = [at(f"pwin{s}", [P, PAD + T], F32, L0 + 50 * KB + 256 + (2 * KB + 256) * s) for s in range(2)]
        pooled = at("pooled", [P, 2, T], F32, L0 + 56 * KB)
        pgw = at("pgw", [P, 2, PG], F32, L0 + 60 * KB)
        ypout = at("ypout", [P, T], F32, L0 + 62 * KB)

        yp_hi = at("yp_hi", [P, PC, T], F32R, L0 + 16 * KB)
        assert B0 == L0 + 32 * KB
        yp_lo = at("yp_lo", [P, PC, T], F32R, L0 + 48 * KB)
        mlraw = at("mlraw", [P, C, P], F32, L0 + 64 * KB)
        ypin = at("ypin", [P, T], F32, L0 + 72 * KB)
        sga = at("sga", [P, T], F32, L0 + 74 * KB)
        sgp = at("sgp", [P, T], F32, L0 + 76 * KB)
        mout = [at(f"mout{s}", [P, T], F32, L0 + 78 * KB + 2 * KB * s) for s in range(2)]
        mtmp = at("mtmp", [P, T], F32, L0 + 82 * KB)

        x1t = at("x1t", [P, C, T], F32, L0)
        s_all = at("s_all", [P, TB, HP, NK], F32, L0 + 32 * KB)
        skrow = at("skrow", [P, HP, P], F32, L0 + 32 * KB)
        skt = at("skt", [P, HP, NK], F32, L0 + 72 * KB)
        mgin = at("mgin", [P, C, T], F32, L0)
        xtin = [at(f"xtin{s}", [P, T], F32, L0 + 44 * KB + 2 * KB * s) for s in range(2)]
        x1c = [at(f"x1c{s}", [P, T], F32, L0 + 48 * KB + 2 * KB * s) for s in range(2)]
        sq3 = [at(f"sqd{s}", [P, T], F32, L0 + 52 * KB + 2 * KB * s) for s in range(2)]
        rstd2 = at("rstd2", [P, T], F32, L0 + 56 * KB)
        h2full = [at(f"h2full{s}", [P, T], F32, L0 + 58 * KB + 2 * KB * s) for s in range(2)]
        qsb = [at(f"qsb{s}", [P, T], F32, L0 + 80 * KB + 2 * KB * s) for s in range(2)]

        aout = [at(f"aout{s}", [P, T], F32, L0 + 64 * KB + 2 * KB * s) for s in range(2)]
        top_all = at("top_all", [P, TB, PH * TOPK], F32, L0 + 68 * KB)
        i_all = at("i_all", [P, TB, PH * TOPK], F32, L0 + 70 * KB)
        j_all = at("j_all", [P, TB, PH * TOPK], F32, L0 + 72 * KB)
        gate_t = at("gate_t", [P, T], F32, L0 + 74 * KB)
        i_t = at("i_t", [P, T], F32, L0 + 76 * KB)
        j_t = at("j_t", [P, T], F32, L0 + 78 * KB)
        t0 = L0 + 6 * KB
        srow = at("srow", [P, 2, NK], F32, t0)
        srow2 = at("srow2", [P, 2, NK], F32, t0 + KB)
        val = at("val", [P, 2, TOPK], F32, t0 + 2 * KB)
        idx = at("idx", [P, 2, TOPK], U32, t0 + 2 * KB + 128)
        idxf = at("idxf", [P, 2, TOPK], F32, t0 + 2 * KB + 256)
        pos = at("pos", [P, TOPK], U32, t0 + 2 * KB + 384)
        posab = at("posab", [P, 2, TOPK], U32, t0 + 2 * KB + 448)
        posf = at("posf", [P, 2, TOPK], F32, t0 + 2 * KB + 576)
        topv = at("topv", [P, TOPK], F32, t0 + 2 * KB + 704)
        cand = at("cand", [P, TOPK, TOPK], F32, t0 + 3 * KB)
        cand2 = at("cand2", [P, TOPK, TOPK], F32, t0 + 4 * KB)
        pick = at("pick", [P, 2, TOPK, TOPK], F32, t0 + 5 * KB)
        pick2 = at("pick2", [P, 2, TOPK, TOPK], F32, t0 + 7 * KB)
        zsum = at("zsum", [P, TB * PH], F32, t0 + 9 * KB)
        GT = 64
        gbuf = [at(f"gbuf{s}", [P, EB, GT], F32, L0 + 32 * KB * s) for s in range(2)]
        oh_j, oh_i, oh_g = ([at(f"{name}{s}", [P, 4, P], F32, L0 + (80, 68)[s] * KB + 2 * KB * k) for s in range(2)]
                            for k, name in enumerate(("oh_j", "oh_i", "oh_g")))

        HALF = D // 2
        HC = HALF // P
        up_raw = [at(f"up_raw{s}", [P, HALF], F32, o + 4 * KB * s) for s in range(2)]
        up_hi = [at(f"up_hi{s}", [P, HALF], F32R, o + 8 * KB + 4 * KB * s) for s in range(2)]
        up_lo = [at(f"up_lo{s}", [P, HALF], F32R, o + 16 * KB + 4 * KB * s) for s in range(2)]
        L1 = L0 + 68 * KB
        a_in = [at(f"a_in{s}", [P, T], F32, L1 + 2 * KB * s) for s in range(2)]
        g_in = [at(f"g_in{s}", [P, T], F32, L1 + 4 * KB + 2 * KB * s) for s in range(2)]
        ag = [at(f"ag{s}", [P, T], F32, L1 + 8 * KB + 2 * KB * s) for s in range(2)]
        ag_hi = [at(f"ag_hi{s}", [P, T], F32R, L1 + 12 * KB + 2 * KB * s) for s in range(2)]
        ag_lo = [at(f"ag_lo{s}", [P, T], F32R, L1 + 16 * KB + 2 * KB * s) for s in range(2)]
        x1f = at("x1f", [P, C, T], F32, L0)
        orow = [at(f"orow{s}", [P, D], F32, L0 + 32 * KB + 8 * KB * s) for s in range(4)]

        bank = [ctx.enter_context(nc.psum_tensor(f"bank{b}", [P, T], F32)) for b in range(8)]
        B_MOD, B_SUM = bank[7], bank[6]

        raw_landed = [sem(f"raw_landed{s}") for s in range(2)]
        raw_seen = sem("raw_seen")
        hi_ready = sem("hi_ready")
        lo_ready = sem("lo_ready")
        unit_done = sem("unit_done")
        z_free = [sem(f"z_free{s}") for s in range(2)]

        def load_unit(sp, u, *parts):
            s = slot(u)
            if not (isinstance(u, int) and u < 2):
                sp.wait_ge(lo_ready, u - 1)
            if len(parts) == 1:
                sp.dma_start(raw[s][:, :, :], parts[0]).then_inc(raw_landed[s], 16)
            else:
                half = C // 2
                sp.sem_inc(raw_seen, 1)
                sp.dma_start(raw[s][:, 0:half, :], parts[0]).then_inc(raw_landed[s], 16)
                sp.dma_start(raw[s][:, half:C, :], parts[1]).then_inc(raw_landed[s], 16)

        parity = {}

        def unit(base, i, step, off):
            u = base + step * i + off
            parity[id(u)] = (u, (base + off) % 2)
            return u

        def slot(u):
            return u % 2 if isinstance(u, int) else parity[id(u)][1]

        def landed(u):
            return u

        def split_hi(act, u, count):
            s = slot(u)
            act.wait_ge(raw_landed[s], 16 * count)
            if not (isinstance(u, int) and u < 2):
                act.wait_ge(unit_done, u - 1)
            act.activation(w_hi_t[s][:, :, :], raw[s][:, :, :], ACT.Copy).then_inc(hi_ready, 1)

        def split_lo(dve, u):
            s = slot(u)
            dve.wait_ge(hi_ready, u + 1)
            dve.tensor_tensor(w_lo_t[s][:, :, :], raw[s][:, :, :], w_hi_t[s][:, :, :].bitcast(F32),
                              ALU.subtract).then_inc(lo_ready, 1)

        def three_pass(pe, dst, s, cw, mh, ml, first, last):
            pe.matmul(dst, w_hi_t[s][:, cw, :], mh, start=first, stop=False)
            pe.matmul(dst, w_hi_t[s][:, cw, :], ml, start=False, stop=False)
            return pe.matmul(dst, w_lo_t[s][:, cw, :], mh, start=False, stop=last)

        def lands(u0):
            n = 0
            for u in range(u0 % 2, u0 + 1, 2):
                n += 2 if U_MIX <= u < U_OUT and (u - U_MIX) % 3 == 2 else 1
            return n

        def lands_in(base, i, step, off):
            a = lands(base + off)
            b = lands(base + off + step)
            return a + (b - a) * i

        io = sem("vectors_landed")
        consts = sem("consts")
        pool_step = sem("pool_step")
        vec_t = sem("vec_t")
        vec_c = sem("vec_c")
        cond_ready = sem("cond_ready")
        mraw_landed = [sem(f"mraw_landed{s}") for s in range(4)]
        mstep = sem("mstep")
        macc_ready = sem("macc_ready")
        msum_done = sem("msum_done")
        mod_ready = sem("mod_ready")
        x_landed = [sem(f"x_landed{s}") for s in range(TB)]
        xtr_done = sem("xtr_done")
        xt_copied = sem("xt_copied")
        xt_stored = sem("xt_stored")
        sq_ready = sem("sq_ready")
        ss_step = sem("ss_step")
        rms_root = sem("rms_root")
        rms_ready = sem("rms_ready")
        xn_ready = sem("xn_ready")

        mix_free = sem("mix_free")
        ml_done = sem("ml_done")
        ml_evac = sem("ml_evac")
        g_done = sem("g_done")
        a_stored = [sem(f"a_stored{s}") for s in range(2)]
        g_stored = [sem(f"g_stored{s}") for s in range(2)]

        NE = 2 * C // 2
        CV = 10

        with nc.Block() as block:
            @block.gpsimd
            def _(pool):
                pool.sem_inc(mix_free, 1)
                pool.memset(ones[:, :], 1.0).then_inc(pool_step, 1)
                pool.memset(ident[:, :], 0.0).then_inc(pool_step, 1)
                pool.memset(blockones[:, :], 0.0).then_inc(pool_step, 1)
                pool.memset(eps[:, :], EPS).then_inc(pool_step, 1)
                pool.wait_ge(pool_step, 4)
                pool.affine_select(out=ident[:, :], in_=ident[:, :], compare_op=ALU.not_equal, fill=1.0,
                                   base=0, pattern=[[-1, P]], channel_multiplier=1).then_inc(consts, 1)
                pool.wait_ge(consts, 1)
                pool.memset(blockones[0:HD, 0:HD], 1.0).then_inc(consts, 1)
                pool.wait_ge(consts, 2)
                pool.memset(blockones[HD:P, HD:P], 1.0).then_inc(consts, 1)
                pool.wait_ge(consts, 3)
                pool.iota(iota_keys[:, :], pattern=[[1, P]], base=0, channel_multiplier=0,
                          allow_small_or_imprecise_dtypes=True).then_inc(consts, 1)
                for g, w in enumerate(WINDOWS):
                    for t in range(16):
                        if t < w - 1:
                            pool.memset(rcount[:, g, t:t + 1], 1.0 / (t + 1)).then_inc(consts, 1)
                    pool.memset(rcount[:, g, w - 1:16], 1.0 / w).then_inc(consts, 1)

            @block.sync
            def _(sp):
                sp.dma_start(vrow_a[0:6 * C, :], b_ada[0].rearrange("(r p) -> r p", p=P)).then_inc(io, 16)
                sp.dma_start(vrow_a[6 * C:7 * C, :], c[0].rearrange("(r p) -> r p", p=P)).then_inc(io, 16)
                sp.dma_start(vrow_a[7 * C:8 * C, :], norm1_g[0].rearrange("(r p) -> r p", p=P)).then_inc(io, 16)
                sp.dma_start(vrow_b[0:C, :], norm2_g[0].rearrange("(r p) -> r p", p=P)).then_inc(io, 16)
                sp.dma_start(vrow_b[C:C + PC, :], pool_scale[0].rearrange("(r p) -> r p", p=P)).then_inc(io, 16)
                for k in range(2):
                    sp.dma_start(vrow_b[C + PC:C + PC + 1, k * HD:(k + 1) * HD], q_norm_g).then_inc(io, 16)
                    sp.dma_start(vrow_b[C + PC + 1:C + PC + 2, k * HD:(k + 1) * HD], k_norm_g).then_inc(io, 16)
                sp.dma_start(sinkrow[0:1, :], attn_sinks).then_inc(io, 16)
                for tb in range(TB):
                    sp.dma_start(xrow[tb][:, :], x[0, tb * P:(tb + 1) * P, :]).then_inc(x_landed[tb], 16)
                for s in range(4):
                    sp.dma_start(mraw[s][:, :, :], w_ada_v[:, :, s * MOD_W:(s + 1) * MOD_W])\
                      .then_inc(mraw_landed[s], 16)

                def four_loads(i):
                    for s in range(4):
                        sp.wait_ge(msum_done, 4 * i + s - 3)
                        sp.dma_start(mraw[s][:, :, :],
                                     w_ada_v[:, :, bass.ds((4 * i + s) * MOD_W, MOD_W)])\
                          .then_inc(mraw_landed[s], 16)

                with sp.Fori(1, NE // 4 - 1) as i:
                    four_loads(i)
                load_unit(sp, 0, w_in_v[:, :, col_of(0):col_of(0) + P])
                load_unit(sp, 1, w_in_v[:, :, col_of(1):col_of(1) + P])
                four_loads(NE // 4 - 1)
                sp.wait_ge(xt_copied, 4 * TB)
                sp.dma_start(xt_dram.rearrange("c p t -> p c t"), xt[:, :, :]).then_inc(xt_stored, 16)

            @block.tensor
            def _(pe):
                pe.wait_ge(consts, 1)
                pe.wait_ge(io, 16 * 10)
                pe.transpose(bank[0][:, 0:P], vrow_a[:, :], ident[:, :])
                pe.transpose(bank[0][:, P:P + 26], vrow_b[0:26, :], ident[0:26, 0:26])
                pe.matmul(bank[0][:, 2 * P:2 * P + NQ], ones[0:1, :], sinkrow[0:1, :],
                          start=True, stop=True).then_inc(vec_t, 1)
                pe.wait_ge(vec_c, 1)

                def mod_sums(i, s):
                    v = 4 * i + s
                    pe.wait_ge(mraw_landed[s], 16 * (i + 1))
                    for k in range(2):
                        cols = slice(k * P, (k + 1) * P)
                        dst = B_MOD[:, bass.ds(2 * v + k, 1)]
                        for cc in range(CV, C):
                            pe.matmul(dst, mraw[s][:, cc, cols], cond[:, cc:cc + 1],
                                      start=(cc == CV), stop=False)
                        if k == 0:
                            pe.wait_ge(macc_ready, v + 1)
                        for e in range(2):
                            mm = pe.matmul(dst, macc_e[s % 2][:, e, cols],
                                           ones[:, 0:1], start=False, stop=(e == 1))
                    mm.then_inc(msum_done, 1)

                pe.wait_ge(cond_ready, 1)
                for tb in range(TB):
                    pe.wait_ge(x_landed[tb], 16)
                    for q in range(4):
                        if tb:
                            pe.wait_ge(xt_copied, 4 * (tb - 1) + q + 1)
                        for r in range(4):
                            cc = 4 * q + r
                            mm = pe.transpose(bank[q][:, r * P:(r + 1) * P],
                                              xrow[tb][:, cc * P:(cc + 1) * P], ident[:, :])
                        mm.then_inc(xtr_done, 1)
                for cc in range(C):
                    pe.wait_ge(sq_ready, cc + 1)
                    pe.matmul(B_SUM[:, :], ones[:, :], sq[cc % 2][:, :], start=(cc == 0),
                              stop=(cc == C - 1)).then_inc(ss_step, 1)
                    if cc % 4 == 3:
                        mod_sums(0, cc // 4)
                with pe.Fori(1, NE // 4) as i:
                    for s in range(4):
                        mod_sums(i, s)

            @block.scalar
            def _(act):
                act.wait_ge(vec_c, 1)
                act.activation(csig[:, :], vec_a[:, 6 * C:7 * C], ACT.Sigmoid).then_inc(vec_c, 1)
                for tb in range(TB):
                    for q in range(4):
                        act.wait_ge(xtr_done, 4 * tb + q + 1)
                        act.activation(xt[:, 4 * q:4 * q + 4, tb * P:(tb + 1) * P],
                                       bank[q][:, :].rearrange("p (r t) -> p r t", r=4),
                                       ACT.Copy).then_inc(xt_copied, 1)
                act.wait_ge(xt_copied, 4 * TB)
                for cc in range(C):
                    if cc >= 2:
                        act.wait_ge(ss_step, cc - 1)
                    act.activation(sq[cc % 2][:, :], xt[:, cc, :], ACT.Square).then_inc(sq_ready, 1)
                act.wait_ge(ss_step, C)
                act.activation(rstd[:, :], B_SUM[:, :], ACT.Sqrt, bias=eps[:, :], scale=1.0 / D)\
                   .then_inc(rms_root, 1)
                act.wait_ge(msum_done, NE - 1)
                split_hi(act, 0, 1)
                split_hi(act, 1, 1)

            @block.vector
            def _(dve):
                dve.wait_ge(vec_t, 1)
                dve.tensor_copy(vec_a[:, :], bank[0][:, 0:P])
                dve.tensor_copy(vec_b[:, 0:26], bank[0][:, P:P + 26])
                dve.tensor_copy(sinks[:, :], bank[0][:, 2 * P:2 * P + NQ]).then_inc(vec_c, 1)
                dve.wait_ge(vec_c, 2)
                dve.tensor_tensor(cond[:, :], vec_a[:, 6 * C:7 * C], csig[:, :], ALU.mult)\
                   .then_inc(cond_ready, 1)
                dve.wait_ge(cond_ready, 1)

                def early(i, s):
                    v = 4 * i + s
                    if not (isinstance(i, int) and v < 2):
                        dve.wait_ge(msum_done, v - 1)
                    dve.wait_ge(mraw_landed[s], 16 * (i + 1))
                    for cc in range(CV):
                        e = cc % 2
                        if cc < 2:
                            ins = dve.tensor_scalar(macc_e[s % 2][:, e, :], mraw[s][:, cc, :],
                                                    cond[:, cc:cc + 1], None, ALU.mult)
                        else:
                            dve.wait_ge(mstep, CV * v + cc - 1)
                            ins = dve.scalar_tensor_tensor(
                                out=macc_e[s % 2][:, e, :], in0=mraw[s][:, cc, :], scalar=cond[:, cc:cc + 1],
                                in1=macc_e[s % 2][:, e, :], op0=ALU.mult, op1=ALU.add)
                        ins.then_inc(mstep, 1)
                    dve.wait_ge(mstep, CV * v + CV)
                    dve.sem_inc(macc_ready, 1)

                def early_four(i):
                    for s in range(4):
                        early(i, s)

                early_four(0)
                early_four(1)
                dve.wait_ge(rms_root, 1)
                dve.reciprocal(rstd[:, :], rstd[:, :]).then_inc(rms_ready, 1)
                dve.wait_ge(rms_ready, 1)
                for cc in range(C):
                    dve.tensor_tensor(xn[:, cc, :], xt[:, cc, :], rstd[:, :], ALU.mult)\
                       .then_inc(xn_ready, 1)
                with dve.Fori(2, NE // 4) as i:
                    early_four(i)
                dve.wait_ge(msum_done, NE)
                dve.tensor_tensor(mod[:, 0:2 * C], B_MOD[:, 0:2 * C], vec_a[:, 0:2 * C],
                                  ALU.add).then_inc(mod_ready, 1)
                dve.wait_ge(mod_ready, 1)
                dve.scalar_tensor_tensor(out=mul1[:, :], in0=mod[:, C:2 * C], scalar=1.0,
                                         in1=vec_a[:, 7 * C:8 * C], op0=ALU.add, op1=ALU.mult)\
                   .then_inc(xn_ready, 1)
                split_lo(dve, 0)
                split_lo(dve, 1)

        h_full = sem("h_full")
        h_hi = sem("h_hi")
        h_ready = sem("h_ready")
        zc_ready = sem("zc_ready")
        zq_ready = sem("zq_ready")
        hs_done = sem("hs_done")
        hr_root = sem("hr_root")
        hr_inv = sem("hr_inv")
        qk_ready = sem("qk_ready")
        kdup_landed = sem("kdup_landed")
        vtr_done = sem("vtr_done")
        v_ready = sem("v_ready")
        mask_ready = sem("mask_ready")
        s_done = sem("s_done")
        s_max = sem("s_max")
        s_shift = sem("s_shift")
        s_stat = sem("s_stat")
        s_exp = sem("s_exp")
        s_esink = sem("s_esink")
        s_sum = sem("s_sum")
        p_ready = sem("p_ready")
        pt_done = sem("pt_done")
        pt_copied = sem("pt_copied")
        o_done = sem("o_done")
        y_hi_done = sem("y_hi_done")
        y_ready = sem("y_ready")
        pin_ready = sem("pin_ready")
        win_step = sem("win_step")
        pooled_ready = sem("pooled_ready")
        pgw_landed = sem("pgw_landed")
        pl_done = sem("pl_done")
        yp_ready = sem("yp_ready")
        yp_stored = sem("yp_stored")
        pad_ready = sem("pad_ready")

        def z_uses(u):
            return u // 2

        def z_unit(pe, u, nuse, cs=None, wait_h=False):
            s = slot(u)
            cs = range(C) if cs is None else cs
            if cs[0] == 0:
                pe.wait_ge(lo_ready, u + 1)
                if not (isinstance(nuse, int) and nuse == 0):
                    pe.wait_ge(z_free[s], nuse)
            for cc in cs:
                if wait_h:
                    pe.wait_ge(h_ready, cc + 1)
                mm = three_pass(pe, bank[s][:, :], s, cc, act_hi[:, cc, :], act_lo[:, cc, :],
                                cc == 0, cc == C - 1)
            if cs[-1] == C - 1:
                mm.then_inc(unit_done, 1)

        GROUPS = [(tb, hg) for tb in range(TB) for hg in range(NQ // 4)]

        with nc.Block() as block:
            @block.sync
            def _(sp):
                for u in range(2, U_MIX):
                    load_unit(sp, u, w_in_v[:, :, col_of(u):col_of(u) + P])
                for u in range(U_MIX, U_MIX + 2):
                    off = AW + 2 * NKV * HD + PW + (u - U_MIX) * D
                    load_unit(sp, u, w_in_v[:, :, off:off + P])

            @block.tensor
            def _(pe):
                def head_sums(j):
                    pe.wait_ge(zq_ready, j + 1)
                    if j:
                        pe.wait_ge(hr_root, j)
                    pe.matmul(B_SUM[:, :], blockones[:, :], sq2[j % 2][:, :], start=True, stop=True)\
                      .then_inc(hs_done, 1)

                for u in range(U_POOL):
                    z_unit(pe, u, z_uses(u), wait_h=(u == 0))
                    if u - 1 in NORMS:
                        head_sums(NORMS.index(u - 1))
                    if u == U_V + 1:
                        pe.wait_ge(zc_ready, U_V + 1)
                        for tb in range(TB):
                            mm = pe.transpose(bank[7][:, tb * P:(tb + 1) * P], vt[:, tb * P:(tb + 1) * P],
                                              ident[:, :])
                        mm.then_inc(vtr_done, 1)

                def scores(n):
                    tb, hg = GROUPS[n]
                    pe.wait_ge(qk_ready, 1 + 2 * hg + 2)
                    if n == 0:
                        pe.wait_ge(kdup_landed, 16 * 2 * NKV)
                    else:
                        pe.wait_ge(s_shift, 2 * n)
                    for r in range(4):
                        h = 4 * hg + r
                        ps = (h % 2) * HD
                        lo = P if tb == 0 else HD
                        mm = pe.matmul(bank[4 + r % 2][:, (r // 2) * 2 * P + lo:(r // 2 + 1) * 2 * P],
                                       qt[ps:ps + HD, h // 2, tb * P:(tb + 1) * P],
                                       kdup[hg // 2][ps:ps + HD, (tb - 1) * P + lo:(tb + 1) * P],
                                       start=True, stop=True)
                    mm.then_inc(s_done, 1)

                def values(n):
                    tb, hg = GROUPS[n]
                    pe.wait_ge(p_ready, n + 1)
                    if n:
                        pe.wait_ge(pt_copied, 2 * n)
                    for b in range(2):
                        for r in range(2):
                            for k in range(2):
                                mm = pe.transpose(bank[2 + b][:, (2 * r + k) * P:(2 * r + k + 1) * P],
                                                  prob[n % 2][:, 2 * b + r, k * P:(k + 1) * P], ident[:, :])
                        mm.then_inc(pt_done, 1)
                    if n == 0:
                        pe.wait_ge(v_ready, 1)
                    else:
                        pe.wait_ge(y_ready, n)
                    pe.wait_ge(pt_copied, 2 * n + 2)
                    kv = hg // 2
                    for r in range(4):
                        ps = (r // 2) * HD
                        dst = B_SUM[ps:ps + HD, (r % 2) * P:(r % 2 + 1) * P]
                        for k in range(2):
                            if tb == 0 and k == 0:
                                continue
                            mm = pe.matmul(dst, vrows[:, tb - 1 + k, kv * HD:(kv + 1) * HD],
                                           prob_t[:, r, k, :], start=(k == 0 or tb == 0), stop=(k == 1))
                    mm.then_inc(o_done, 1)

                def pool_linear(g):
                    pe.wait_ge(pooled_ready, 2 * g + 2)
                    pe.wait_ge(pgw_landed, 16 * (g + 1))
                    for m in range(2):
                        n = 2 * g + m
                        if n == 0:
                            pe.wait_ge(v_ready, 1)
                        else:
                            pe.wait_ge(yp_ready, n)
                        for k in range(2):
                            mm = pe.matmul(bank[7][:, :], pgw[:, k, m * P:(m + 1) * P], pooled[:, k, :],
                                           start=(k == 0), stop=(k == 1))
                        mm.then_inc(pl_done, 1)

                for p in range(PC):
                    u = U_POOL + p
                    for k in range(2):
                        n = 2 * p + k
                        scores(n)
                        if n == 0:
                            head_sums(len(NORMS) - 1)
                        z_unit(pe, u, z_uses(u), cs=range(k * C // 2, (k + 1) * C // 2))
                        if n:
                            values(n - 1)
                    if p % 2 == 0 and p:
                        pool_linear(p // 2 - 1)
                values(2 * PC - 1)
                pool_linear(NG - 1)

            @block.scalar
            def _(act):
                act.wait_ge(xn_ready, C + 1)
                for cc in range(C):
                    act.activation(act_hi[:, cc, :], xn[:, cc, :], ACT.Identity, bias=mod[:, cc:cc + 1],
                                   scale=mul1[:, cc:cc + 1]).then_inc(h_hi, 1)

                def head_root(j):
                    act.wait_ge(hs_done, j + 1)
                    if j >= 2:
                        act.wait_ge(qk_ready, j - 1)
                    act.activation(rq[j % 2][:, :], B_SUM[:, :], ACT.Sqrt, bias=eps[:, :],
                                   scale=1.0 / HD).then_inc(hr_root, 1)

                for u in range(U_POOL):
                    s = u % 2
                    if u:
                        split_hi(act, u + 1, lands(u + 1))
                    act.wait_ge(unit_done, u + 1)
                    dst = qt[:, u - U_Q, :] if u >= U_Q else (kt, vt)[u][:, :]
                    act.activation(dst, bank[s][:, :], ACT.Copy).then_inc(zc_ready, 1)
                    if u in NORMS:
                        j = NORMS.index(u)
                        if j >= 2:
                            act.wait_ge(hs_done, j - 1)
                        act.activation(sq2[j % 2][:, :], bank[s][:, :], ACT.Square).then_inc(zq_ready, 1)
                        act.wait_ge(zq_ready, j + 1)
                    act.wait_ge(zc_ready, u + 1)
                    act.sem_inc(z_free[s], 1)
                    if u - 1 in NORMS:
                        head_root(NORMS.index(u - 1))
                head_root(len(NORMS) - 1)

                def softmax_exp(n):
                    act.wait_ge(s_shift, 2 * n + 2)
                    if n >= 2:
                        act.wait_ge(pt_done, 2 * n - 2)
                    act.activation(prob[n % 2][:, :, :], sprob[:, :, :], ACT.Exp).then_inc(s_exp, 1)
                    act.wait_ge(s_stat, 2 * n + 2)
                    act.activation(stat[:, 3, :], stat[:, 2, :], ACT.Exp).then_inc(s_esink, 1)

                def copy_probs(n):
                    for b in range(2):
                        act.wait_ge(pt_done, 2 * n + b + 1)
                        if n:
                            act.wait_ge(o_done, n)
                        act.activation(prob_t[:, 2 * b:2 * b + 2, :, :],
                                       bank[2 + b][:, :].rearrange("p (r k t) -> p r k t", r=2, k=2),
                                       ACT.Copy).then_inc(pt_copied, 1)

                def y_high(n):
                    tb, hg = GROUPS[n]
                    act.wait_ge(o_done, n + 1)
                    act.activation(y_hi[:, 2 * hg:2 * hg + 2, tb * P:(tb + 1) * P],
                                   B_SUM[:, 0:2 * P].rearrange("p (r t) -> p r t", r=2),
                                   ACT.Copy).then_inc(y_hi_done, 1)

                def pool_in(p):
                    u = U_POOL + p
                    s = u % 2
                    act.wait_ge(unit_done, u + 1)
                    if p:
                        act.wait_ge(pooled_ready, p)
                    else:
                        act.wait_ge(pad_ready, 1)
                    act.activation(pin[:, PAD:], bank[s][:, :], ACT.Copy).then_inc(pin_ready, 1)
                    act.wait_ge(pin_ready, p + 1)
                    act.sem_inc(z_free[s], 1)

                for p in range(PC):
                    u = U_POOL + p
                    softmax_exp(2 * p)
                    split_hi(act, u + 1, lands(u + 1))
                    if p:
                        copy_probs(2 * p - 1)
                        y_high(2 * p - 1)
                    softmax_exp(2 * p + 1)
                    pool_in(p)
                    copy_probs(2 * p)
                    y_high(2 * p)
                copy_probs(2 * PC - 1)
                y_high(2 * PC - 1)

            @block.vector
            def _(dve):
                def h_low(cc):
                    dve.wait_ge(h_full, cc + 1)
                    dve.wait_ge(h_hi, cc + 1)
                    dve.tensor_tensor(act_lo[:, cc, :], hfull[cc % 2][:, :], act_hi[:, cc, :].bitcast(F32),
                                      ALU.subtract).then_inc(h_ready, 1)

                dve.wait_ge(xn_ready, C + 1)
                for cc in range(C):
                    if cc >= 2:
                        dve.wait_ge(h_ready, cc - 1)
                    dve.tensor_scalar(hfull[cc % 2][:, :], xn[:, cc, :], mul1[:, cc:cc + 1],
                                      mod[:, cc:cc + 1], ALU.mult, ALU.add).then_inc(h_full, 1)
                    if cc:
                        h_low(cc - 1)
                h_low(C - 1)

                def normalise(j):
                    dve.wait_ge(hr_root, j + 1)
                    dve.reciprocal(rq[j % 2][:, :], rq[j % 2][:, :]).then_inc(hr_inv, 1)
                    dve.wait_ge(hr_inv, j + 1)
                    dve.wait_ge(zc_ready, NORMS[j] + 1)
                    z = qt[:, j - 1, :] if j else kt[:, :]
                    col = C + PC + (j == 0)
                    dve.scalar_tensor_tensor(out=z, in0=z, scalar=vec_b[:, col:col + 1],
                                             in1=rq[j % 2][:, :], op0=ALU.mult, op1=ALU.mult)\
                       .then_inc(qk_ready, 1)

                for u in range(U_POOL):
                    if u:
                        split_lo(dve, u + 1)
                        if u - 1 in NORMS:
                            normalise(NORMS.index(u - 1))
                    if u == U_V + 1:
                        dve.wait_ge(vtr_done, 1)
                        dve.tensor_copy(vrows[:, :, :], bank[7][:, :].rearrange("p (b d) -> p b d", b=TB))\
                           .then_inc(v_ready, 1)

                def by_bank(v):
                    return v.rearrange("p (b r) -> p b r", b=2)

                def sinks_of(hg):
                    return sinks[:, 4 * hg:4 * hg + 4].rearrange("p (r b) -> p b r", b=2)

                def softmax_max(n):
                    tb, hg = GROUPS[n]
                    dve.wait_ge(s_done, n + 1)
                    spans = [(0, P if tb == 0 else HD, P + HD), (HD, P, 2 * P)]
                    for half, (ps, lo, hi) in enumerate(spans):
                        for b in range(2):
                            ins = dve.tensor_reduce(
                                stat[ps:ps + HD, 0, 2 * b:2 * b + 2],
                                bank[4 + b][ps:ps + HD, :].rearrange("p (r m) -> p r m", r=2)[:, :, lo:hi],
                                AX.X, ALU.max)
                    ins.then_inc(s_max, 1)
                    dve.wait_ge(s_max, 2 * n + 1)
                    dve.scalar_tensor_tensor(out=by_bank(stat[:, 1, :]), in0=by_bank(stat[:, 0, :]),
                                             scalar=SCALE, in1=sinks_of(hg), op0=ALU.mult, op1=ALU.max)\
                       .then_inc(s_max, 1)
                    dve.wait_ge(s_max, 2 * n + 2)
                    if n:
                        dve.wait_ge(s_exp, n)
                    for b in range(2):
                        for half, (ps, lo, hi) in enumerate(spans):
                            ins = dve.scalar_tensor_tensor(
                                out=sprob[ps:ps + HD, 2 * b:2 * b + 2, lo:hi],
                                in0=bank[4 + b][ps:ps + HD, :].rearrange("p (r m) -> p r m", r=2)[:, :, lo:hi],
                                scalar=SCALE,
                                in1=stat[ps:ps + HD, 1, 2 * b:2 * b + 2].unsqueeze(2).to_broadcast([HD, 2, hi - lo]),
                                op0=ALU.mult, op1=ALU.subtract)
                        ins.then_inc(s_shift, 1)
                    if n:
                        dve.wait_ge(s_esink, n)
                    dve.tensor_tensor(by_bank(stat[:, 2, :]), sinks_of(hg), by_bank(stat[:, 1, :]),
                                      ALU.subtract).then_inc(s_stat, 2)

                def softmax_norm(n):
                    dve.wait_ge(s_exp, n + 1)
                    dve.wait_ge(s_esink, n + 1)
                    dve.tensor_reduce(stat[:, 4, :], prob[n % 2][:, :, :], AX.X, ALU.add).then_inc(s_sum, 1)
                    dve.wait_ge(s_sum, 3 * n + 1)
                    dve.tensor_tensor(stat[:, 4, :], stat[:, 4, :], stat[:, 3, :], ALU.add).then_inc(s_sum, 1)
                    dve.wait_ge(s_sum, 3 * n + 2)
                    dve.reciprocal(stat[:, 5, :], stat[:, 4, :]).then_inc(s_sum, 1)
                    dve.wait_ge(s_sum, 3 * n + 3)
                    dve.tensor_tensor(prob[n % 2][:, :, :], prob[n % 2][:, :, :],
                                      stat[:, 5, :].unsqueeze(2).to_broadcast([P, 4, 2 * P]),
                                      ALU.mult).then_inc(p_ready, 1)

                def y_low(n):
                    tb, hg = GROUPS[n]
                    dve.wait_ge(y_hi_done, n + 1)
                    dve.tensor_tensor(y_lo[:, 2 * hg:2 * hg + 2, tb * P:(tb + 1) * P],
                                      B_SUM[:, 0:2 * P].rearrange("p (r t) -> p r t", r=2),
                                      y_hi[:, 2 * hg:2 * hg + 2, tb * P:(tb + 1) * P].bitcast(F32),
                                      ALU.subtract).then_inc(y_ready, 1)

                def pool_out(g):
                    for m in range(2):
                        n = 2 * g + m
                        dve.wait_ge(pl_done, n + 1)
                        if n:
                            dve.wait_ge(yp_stored, 16 * n)
                        dve.tensor_scalar(ypout[:, :], bank[7][:, :], vec_b[:, C + n:C + n + 1], None,
                                          ALU.mult).then_inc(yp_ready, 1)

                dve.wait_ge(xt_stored, 16)
                dve.memset(sprob[:, :, :], -1.0e30).then_inc(mask_ready, 1)
                dve.wait_ge(mask_ready, 1)
                for p in range(PC):
                    u = U_POOL + p
                    softmax_max(2 * p)
                    if p == 0:
                        normalise(len(NORMS) - 1)
                    split_lo(dve, u + 1)
                    softmax_norm(2 * p)
                    if p:
                        y_low(2 * p - 1)
                    softmax_max(2 * p + 1)
                    softmax_norm(2 * p + 1)
                    y_low(2 * p)
                    if p % 2 == 0 and p:
                        pool_out(p // 2 - 1)
                y_low(2 * PC - 1)
                pool_out(NG - 1)

            @block.gpsimd
            def _(pool):
                pool.wait_ge(qk_ready, 1)
                for k in range(NKV):
                    for half in range(2):
                        pool.dma_start(kdup[k][half * HD:(half + 1) * HD, :],
                                       kt[k * HD:(k + 1) * HD, :]).then_inc(kdup_landed, 16)
                pool.memset(pin[:, 0:PAD], 0.0)
                pool.memset(pwin[0][:, 0:PAD], 0.0)
                pool.memset(pwin[1][:, 0:PAD], 0.0).then_inc(pad_ready, 1)
                def load_linear(g):
                    pool.dma_start(pgw[:, :, :], pool_group_w[0, g].rearrange("(c p) n -> p c n", p=P))\
                        .then_inc(pgw_landed, 16)

                def store_pooled(g):
                    for n in range(2 * g, 2 * g + 2):
                        pool.wait_ge(yp_ready, n + 1)
                        pool.dma_start(ypool_dram[n], ypout[:, :]).then_inc(yp_stored, 16)

                load_linear(0)
                step = 0
                for p in range(PC):
                    g, w = p // 2, WINDOWS[p // 2]
                    if g and p % 2:
                        store_pooled(g - 1)
                        load_linear(g)
                    pool.wait_ge(pin_ready, p + 1)
                    src, k, n = pin, 1, 0
                    while k < w:
                        dst = pwin[n % 2]
                        pool.tensor_tensor(dst[:, PAD:], src[:, PAD:], src[:, PAD - k:PAD - k + T],
                                           ALU.add).then_inc(win_step, 1)
                        step += 1
                        pool.wait_ge(win_step, step)
                        src, k, n = dst, 2 * k, n + 1
                    pool.tensor_tensor(src[:, PAD:PAD + 16], src[:, PAD:PAD + 16], rcount[:, g, :],
                                       ALU.mult).then_inc(win_step, 1)
                    pool.tensor_scalar(src[:, PAD + 16:], src[:, PAD + 16:], 1.0 / w, None,
                                       ALU.mult).then_inc(win_step, 1)
                    step += 2
                    pool.wait_ge(win_step, step)
                    if p >= 2:
                        pool.wait_ge(pl_done, 2 * g)
                    pool.tensor_tensor(pooled[:, p % 2, :], src[:, PAD:], pin[:, PAD:], ALU.subtract)\
                        .then_inc(pooled_ready, 1)
                store_pooled(NG - 1)
                pool.wait_ge(yp_stored, 16 * PC)

        yp_landed = sem("yp_landed")
        yp_hi_done = sem("yp_hi_done")
        yp_halves = sem("yp_halves")
        sig_ready = sem("sig_ready")
        mix_step = sem("mix_step")
        m_ready = sem("m_ready")
        m_stored = [sem(f"m_stored{s}") for s in range(2)]
        ml_landed = sem("ml_landed")
        ml_step = sem("ml_step")
        OFF_GA = AW + 2 * NKV * HD + PW

        def late_sums(dve, v, e0):
            dve.wait_ge(ml_landed, 16 * (v + 1))
            if not (isinstance(v, int) and v < 2):
                dve.wait_ge(ml_done, v - 1)
            for cc in range(C):
                e = cc % 2
                if cc < 2:
                    ins = dve.tensor_scalar(macc[:, e0, e, :], mlraw[:, cc, :], cond[:, cc:cc + 1], None,
                                            ALU.mult)
                else:
                    dve.wait_ge(ml_step, C * v + cc - 1)
                    ins = dve.scalar_tensor_tensor(out=macc[:, e0, e, :], in0=mlraw[:, cc, :],
                                                   scalar=cond[:, cc:cc + 1], in1=macc[:, e0, e, :],
                                                   op0=ALU.mult, op1=ALU.add)
                ins.then_inc(ml_step, 1)

        def late_column(dve, v):
            dve.wait_ge(ml_done, v + 1)
            dve.tensor_tensor(mod[:, bass.ds(2 * C + v, 1)], B_MOD[:, 0:1],
                              vec_a[:, bass.ds(2 * C + v, 1)], ALU.add).then_inc(ml_evac, 1)

        def late_pe(pe, v, e0):
            pe.wait_ge(ml_step, C * v + C)
            if not (isinstance(v, int) and v == 0):
                pe.wait_ge(ml_evac, v)
            for e in range(2):
                mm = pe.matmul(B_MOD[:, 0:1], macc[:, e0, e, :], ones[:, 0:1], start=(e == 0), stop=(e == 1))
            mm.then_inc(ml_done, 1)

        def late_load(sp, v):
            if not (isinstance(v, int) and v == 0):
                sp.wait_ge(ml_step, C * v)
            sp.dma_start(mlraw[:, :, :], w_ada_v[:, :, bass.ds((2 * C + v) * P, P)]).then_inc(ml_landed, 16)

        with nc.Block() as block:
            @block.sync
            def _(sp):
                late_load(sp, 0)
                for n in range(PC):
                    if n:
                        sp.wait_ge(yp_halves, n)
                    sp.dma_start(ypin[:, :], ypool_dram[n]).then_inc(yp_landed, 16)

                def mix_loads(m, first=False):
                    for r in range(2):
                        for k in range(3):
                            off = 3 * r + k
                            u = unit(U_MIX, m, 6, off)
                            if first and off < 2:
                                continue
                            col = (2 * m + r) * P
                            if k < 2:
                                load_unit(sp, u, w_in_v[:, :, bass.ds(OFF_GA + k * D + col, P)])
                            else:
                                load_unit(sp, u, wba_v[:, :, bass.ds(col, P)], wbp_v[:, :, bass.ds(col, P)])
                            if not (first and off == 2):
                                late_load(sp, 6 * m + off - 2)

                mix_loads(0, first=True)
                with sp.Fori(1, C // 2) as m:
                    mix_loads(m)
                for k in range(2):
                    load_unit(sp, U_OUT + k, w_out_v[:, :, k * P:(k + 1) * P])
                    late_load(sp, 3 * C - 2 + k)

            @block.gpsimd
            def _(pool):
                with pool.Fori(0, C // 2) as m:
                    for r in range(2):
                        pool.wait_ge(m_ready, 2 * m + r + 1)
                        pool.dma_start(merged_dram[bass.ds(2 * m + r, 1)].rearrange("a p t -> p (a t)"),
                                       mout[r][:, :]).then_inc(m_stored[r], 16)
                for r in range(2):
                    pool.wait_ge(m_stored[r], 16 * (C // 2))

            @block.tensor
            def _(pe):
                def mix(m, first=False):
                    for r in range(2):
                        n = 2 * m + r
                        for k in range(2):
                            off = 3 * r + k
                            u = unit(U_MIX, m, 6, off)
                            z_unit(pe, u, U_MIX // 2 + 2 * m + r)
                            if not (first and off == 0):
                                late_pe(pe, 6 * m + off - 1, (off - 1) % 2)
                        u = unit(U_MIX, m, 6, 3 * r + 2)
                        s = slot(u)
                        pe.wait_ge(lo_ready, u + 1)
                        pe.wait_ge(mix_free, n + 1)
                        for cc in range(QC):
                            three_pass(pe, bank[2][:, :], s, cc, y_hi[:, cc, :], y_lo[:, cc, :],
                                       cc == 0, cc == QC - 1)
                        pe.wait_ge(yp_halves, PC)
                        for cc in range(PC):
                            mm = three_pass(pe, bank[3][:, :], s, QC + cc, yp_hi[:, cc, :], yp_lo[:, cc, :],
                                            cc == 0, cc == PC - 1)
                        mm.then_inc(unit_done, 1)
                        late_pe(pe, 6 * m + 3 * r + 1, (3 * r + 1) % 2)

                mix(0, first=True)
                with pe.Fori(1, C // 2) as m:
                    mix(m)
                late_pe(pe, 3 * C - 1, 1)

            @block.scalar
            def _(act):
                def mix(m, first=False):
                    for r in range(2):
                        n = 2 * m + r
                        for k in range(3):
                            off = 3 * r + k
                            u = unit(U_MIX, m, 6, off)
                            split_hi(act, unit(U_MIX, m, 6, off + 1), lands_in(U_MIX, m, 6, off + 1))
                            if first and off == 0:
                                for j in range(PC):
                                    act.wait_ge(yp_landed, 16 * (j + 1))
                                    act.activation(yp_hi[:, j, :], ypin[:, :], ACT.Copy).then_inc(yp_hi_done, 1)
                            if k < 2:
                                act.wait_ge(unit_done, u + 1)
                                act.wait_ge(mix_free, n + 1)
                                act.activation((sga, sgp)[k][:, :], bank[slot(u)][:, :], ACT.Sigmoid)\
                                   .then_inc(sig_ready, 1)
                                act.wait_ge(sig_ready, 2 * n + k + 1)
                                act.sem_inc(z_free[slot(u)], 1)

                mix(0, first=True)
                with act.Fori(1, C // 2) as m:
                    mix(m)

            @block.vector
            def _(dve):
                def mix(m, first=False):
                    for r in range(2):
                        n = 2 * m + r
                        for k in range(3):
                            off = 3 * r + k
                            u = unit(U_MIX, m, 6, off)
                            v = 6 * m + off
                            split_lo(dve, unit(U_MIX, m, 6, off + 1))
                            if first and off == 0:
                                for j in range(PC):
                                    dve.wait_ge(yp_hi_done, j + 1)
                                    dve.tensor_tensor(yp_lo[:, j, :], ypin[:, :], yp_hi[:, j, :].bitcast(F32),
                                                      ALU.subtract).then_inc(yp_halves, 1)
                            if not (first and off < 2):
                                late_column(dve, v - 2)
                            late_sums(dve, v, off % 2)
                        u = unit(U_MIX, m, 6, 3 * r + 2)
                        dve.wait_ge(unit_done, u + 1)
                        dve.wait_ge(sig_ready, 2 * n + 2)
                        if not first:
                            dve.wait_ge(m_stored[r], 16 * m)
                        dve.tensor_tensor(mout[r][:, :], sga[:, :], bank[2][:, :], ALU.mult).then_inc(mix_step, 1)
                        dve.tensor_tensor(mtmp[:, :], sgp[:, :], bank[3][:, :], ALU.mult).then_inc(mix_step, 1)
                        dve.wait_ge(mix_step, 2 * n + 2)
                        dve.sem_inc(mix_free, 1)
                        dve.tensor_tensor(mout[r][:, :], mout[r][:, :], mtmp[:, :], ALU.add).then_inc(m_ready, 1)
                        dve.wait_ge(m_ready, n + 1)

                mix(0, first=True)
                with dve.Fori(1, C // 2) as m:
                    mix(m)
                late_column(dve, 3 * C - 2)
                late_column(dve, 3 * C - 1)

        mg_landed = [sem(f"mg_landed{q}") for q in range(4)]
        mg_hi = sem("mg_hi")
        mg_ready = sem("mg_ready")
        xin_landed = [sem(f"xin_landed{s}") for s in range(2)]
        x1_ready = sem("x1_ready")
        x1_kept = sem("x1_kept")
        x1_stored = [sem(f"x1_stored{s}") for s in range(2)]
        x1_sq = sem("x1_sq")
        x1_ss = sem("x1_ss")
        r2_root = sem("r2_root")
        r2_ready = sem("r2_ready")
        h2_full = sem("h2_full")
        h2_hi = sem("h2_hi")
        h2_ready = sem("h2_ready")
        sk_landed = sem("sk_landed")
        sk_tr = sem("sk_tr")
        sk_ready = sem("sk_ready")
        q_ready = sem("q_ready")
        sc_done = sem("sc_done")
        sc_ready = sem("sc_ready")
        mul2_ready = sem("mul2_ready")
        Z_OUT = U_MIX // 2 + C
        down_v = expert_down[0].rearrange("(b p) d -> b p d", p=P)
        down_landed = [sem(f"down_landed{s}") for s in range(2)]

        with nc.Block() as block:
            @block.sync
            def _(sp):
                for q in range(4):
                    sp.dma_start(mgin[:, 4 * q:4 * q + 4, :],
                                 merged_dram[4 * q:4 * q + 4].rearrange("c p t -> p c t")).then_inc(mg_landed[q], 16)
                sp.dma_start(skrow[:, :, :], sub_keys[0].rearrange("h s k d -> k (h s) d")).then_inc(sk_landed, 16)

                def outs(m, first=False):
                    for s in range(2):
                        n = 2 * m + s
                        if not first:
                            load_unit(sp, unit(U_OUT, m, 2, s), w_out_v[:, :, bass.ds(n * P, P)])
                            sp.wait_ge(x1_ready, n - 1)
                        sp.dma_start(xtin[s][:, :], xt_dram[bass.ds(n, 1)].rearrange("a p t -> p (a t)"))\
                          .then_inc(xin_landed[s], 16)

                outs(0, first=True)
                with sp.Fori(1, C // 2) as m:
                    outs(m)

                def queries(m, first=False):
                    for s in range(2):
                        u = unit(U_QRY, m, 2, s)
                        load_unit(sp, u, w_query_v[:, :, bass.ds((2 * m + s) * P, P)])
                        if not first:
                            late_load(sp, 3 * C + 2 * m + s - 2)

                queries(0, first=True)
                with sp.Fori(1, HP // 2) as m:
                    queries(m)
                for s in range(2):
                    late_load(sp, 4 * C - 2 + s)
                for s in range(2):
                    sp.wait_ge(lo_ready, U_END - 1 + s)
                    sp.dma_start(raw[s][:, :, :], down_v[s].rearrange("p (c d) -> p c d", c=C))\
                      .then_inc(down_landed[s], 16)

            @block.tensor
            def _(pe):
                def outs(m, first=False):
                    for s in range(2):
                        n = 2 * m + s
                        u = unit(U_OUT, m, 2, s)
                        pe.wait_ge(lo_ready, u + 1)
                        pe.wait_ge(z_free[s], Z_OUT + m)
                        for cc in range(C):
                            if first and s == 0:
                                pe.wait_ge(mg_ready, cc + 1)
                            mm = three_pass(pe, bank[s][:, :], s, cc, act_hi[:, cc, :], act_lo[:, cc, :],
                                            cc == 0, cc == C - 1)
                        mm.then_inc(unit_done, 1)
                        if not (first and s == 0):
                            squares(n - 1, 1 - s, first and s == 1, False)

                def squares(n, s, start, stop):
                    pe.wait_ge(x1_sq, n + 1)
                    pe.matmul(B_SUM[:, :], ones[:, :], sq3[s][:, :], start=start, stop=stop,
                              skip_group_check=True).then_inc(x1_ss, 1)

                outs(0, first=True)
                pe.wait_ge(sk_landed, 16)
                for q in range(4):
                    for r in range(4):
                        mm = pe.transpose(bank[2 + q][:, r * P:(r + 1) * P], skrow[:, 4 * q + r, :], ident[:, :])
                    mm.then_inc(sk_tr, 1)
                with pe.Fori(1, C // 2) as m:
                    outs(m)
                squares(C - 1, 1, False, True)

                def sub_scores(m, s):
                    n = 2 * m + s
                    pe.wait_ge(q_ready, n + 1)
                    pe.wait_ge(sc_ready, n)
                    for tb in range(TB):
                        mm = pe.matmul(bank[2][:, tb * P:(tb + 1) * P], qsb[s][:, tb * P:(tb + 1) * P],
                                       skt[:, bass.ds(n, 1), :].rearrange("p a k -> p (a k)"),
                                       start=True, stop=True)
                    mm.then_inc(sc_done, 1)

                def queries(m, first=False):
                    for s in range(2):
                        u = unit(U_QRY, m, 2, s)
                        pe.wait_ge(lo_ready, u + 1)
                        pe.wait_ge(z_free[s], Z_OUT + C // 2 + m)
                        for cc in range(C):
                            if first and s == 0:
                                pe.wait_ge(h2_ready, cc + 1)
                            mm = three_pass(pe, bank[s][:, :], s, cc, act_hi[:, cc, :], act_lo[:, cc, :],
                                            cc == 0, cc == C - 1)
                        mm.then_inc(unit_done, 1)
                        if not (first and s == 0):
                            late_pe(pe, 3 * C + 2 * m + s - 1, 1 - s)
                        if first and s == 0:
                            pe.wait_ge(sk_ready, 4)
                        else:
                            sub_scores(m if s else m - 1, 1 - s)

                queries(0, first=True)
                with pe.Fori(1, HP // 2) as m:
                    queries(m)
                sub_scores(HP // 2 - 1, 1)
                late_pe(pe, 4 * C - 1, 1)

            @block.scalar
            def _(act):
                for cc in range(C):
                    act.wait_ge(mg_landed[cc // 4], 16)
                    act.activation(act_hi[:, cc, :], mgin[:, cc, :], ACT.Copy).then_inc(mg_hi, 1)

                def outs(m, first=False):
                    for s in range(2):
                        n = 2 * m + s
                        split_hi(act, unit(U_OUT, m, 2, s + 1), lands_in(U_OUT, m, 2, s + 1))
                        act.wait_ge(x1_ready, n + 1)
                        if not first:
                            act.wait_ge(x1_ss, n - 1)
                        act.activation(sq3[s][:, :], x1c[s][:, :], ACT.Square).then_inc(x1_sq, 1)

                outs(0, first=True)
                for q in range(4):
                    act.wait_ge(sk_tr, q + 1)
                    act.activation(skt[:, 4 * q:4 * q + 4, :], bank[2 + q][:, :].rearrange("p (r k) -> p r k", r=4),
                                   ACT.Copy).then_inc(sk_ready, 1)
                with act.Fori(1, C // 2) as m:
                    outs(m)
                act.wait_ge(x1_ss, C)
                act.activation(rstd2[:, :], B_SUM[:, :], ACT.Sqrt, bias=eps[:, :], scale=1.0 / D)\
                   .then_inc(r2_root, 1)
                for cc in range(C):
                    act.wait_ge(h2_full, cc + 1)
                    act.activation(act_hi[:, cc, :], h2full[cc % 2][:, :], ACT.Identity,
                                   bias=mod[:, 3 * C + cc:3 * C + cc + 1]).then_inc(h2_hi, 1)

                def queries(m, first=False, last=False):
                    for s in range(2):
                        n = 2 * m + s
                        u = unit(U_QRY, m, 2, s)
                        if not (last and s == 1):
                            split_hi(act, unit(U_QRY, m, 2, s + 1), lands_in(U_QRY, m, 2, s + 1))
                        act.wait_ge(unit_done, u + 1)
                        if not first:
                            act.wait_ge(sc_done, n - 1)
                        act.activation(qsb[s][:, :], bank[s][:, :], ACT.Copy).then_inc(q_ready, 1)
                        act.wait_ge(q_ready, n + 1)
                        act.sem_inc(z_free[s], 1)

                queries(0, first=True)
                with act.Fori(1, HP // 2 - 1) as m:
                    queries(m)
                queries(HP // 2 - 1, last=True)

            @block.vector
            def _(dve):
                for cc in range(C):
                    dve.wait_ge(mg_hi, cc + 1)
                    dve.tensor_tensor(act_lo[:, cc, :], mgin[:, cc, :], act_hi[:, cc, :].bitcast(F32),
                                      ALU.subtract).then_inc(mg_ready, 1)

                def outs(m, first=False):
                    for s in range(2):
                        n = 2 * m + s
                        u = unit(U_OUT, m, 2, s)
                        split_lo(dve, unit(U_OUT, m, 2, s + 1))
                        if not first:
                            dve.wait_ge(x1_stored[s], 16 * m)
                            dve.wait_ge(x1_sq, n - 1)
                            dve.wait_ge(x1_kept, n - 1)
                        dve.wait_ge(unit_done, u + 1)
                        dve.wait_ge(xin_landed[s], 16 * m + 16)
                        dve.scalar_tensor_tensor(out=x1c[s][:, :], in0=bank[s][:, :],
                                                 scalar=mod[:, bass.ds(2 * C + n, 1)], in1=xtin[s][:, :],
                                                 op0=ALU.mult, op1=ALU.add).then_inc(x1_ready, 1)
                        dve.wait_ge(x1_ready, n + 1)
                        dve.sem_inc(z_free[s], 1)

                outs(0, first=True)
                with dve.Fori(1, C // 2) as m:
                    outs(m)
                dve.scalar_tensor_tensor(out=mul2[:, :], in0=mod[:, 4 * C:5 * C], scalar=1.0,
                                         in1=vec_b[:, 0:C], op0=ALU.add, op1=ALU.mult).then_inc(mul2_ready, 1)
                dve.wait_ge(r2_root, 1)
                dve.reciprocal(rstd2[:, :], rstd2[:, :]).then_inc(r2_ready, 1)
                dve.wait_ge(r2_ready, 1)
                dve.wait_ge(mul2_ready, 1)
                dve.wait_ge(x1_kept, C)
                dve.wait_ge(unit_done, U_QRY)

                def h2_low(cc):
                    dve.wait_ge(h2_hi, cc + 1)
                    dve.scalar_tensor_tensor(out=act_lo[:, cc, :], in0=h2full[cc % 2][:, :],
                                             scalar=mod[:, 3 * C + cc:3 * C + cc + 1],
                                             in1=act_hi[:, cc, :].bitcast(F32), op0=ALU.add,
                                             op1=ALU.subtract).then_inc(h2_ready, 1)

                for cc in range(C):
                    if cc >= 2:
                        dve.wait_ge(h2_ready, cc - 1)
                    dve.scalar_tensor_tensor(out=h2full[cc % 2][:, :], in0=x1t[:, cc, :],
                                             scalar=mul2[:, cc:cc + 1], in1=rstd2[:, :], op0=ALU.mult,
                                             op1=ALU.mult).then_inc(h2_full, 1)
                    if cc:
                        h2_low(cc - 1)
                h2_low(C - 1)

                def take_scores(m, s):
                    n = 2 * m + s
                    dve.wait_ge(sc_done, n + 1)
                    dve.tensor_scalar(s_all[:, :, bass.ds(n, 1), :].rearrange("p b a k -> p b (a k)"),
                                      bank[2][:, :].rearrange("p (b k) -> p b k", b=TB), 1.0, None,
                                      ALU.mult).then_inc(sc_ready, 1)

                def queries(m, first=False, last=False):
                    for s in range(2):
                        v = 3 * C + 2 * m + s
                        if not (last and s == 1):
                            split_lo(dve, unit(U_QRY, m, 2, s + 1))
                        if not first:
                            late_column(dve, v - 2)
                        late_sums(dve, v, s)
                        if not (first and s == 0):
                            take_scores(m if s else m - 1, 1 - s)

                dve.wait_ge(sk_ready, 4)
                for s in range(2):
                    dve.wait_ge(x1_stored[s], 16 * (C // 2))
                queries(0, first=True)
                with dve.Fori(1, HP // 2 - 1) as m:
                    queries(m)
                queries(HP // 2 - 1, last=True)
                take_scores(HP // 2 - 1, 1)
                late_column(dve, 4 * C - 2)
                late_column(dve, 4 * C - 1)

            @block.gpsimd
            def _(pool):
                def keep(m):
                    for s in range(2):
                        n = 2 * m + s
                        pool.wait_ge(x1_ready, n + 1)
                        pool.dma_start(x1_dram[bass.ds(n, 1)].rearrange("a p t -> p (a t)"), x1c[s][:, :])\
                            .then_inc(x1_stored[s], 16)
                        pool.tensor_copy(x1t[:, bass.ds(n, 1), :].rearrange("p a t -> p (a t)"), x1c[s][:, :])\
                            .then_inc(x1_kept, 1)

                with pool.Fori(0, C // 2) as m:
                    keep(m)
                for s in range(2):
                    pool.wait_ge(x1_stored[s], 16 * (C // 2))

        dtr_done = sem("dtr_done")
        d_hi = sem("d_hi")
        d_lo = sem("d_lo")
        a_done = sem("a_done")
        a_ready = sem("a_ready")
        tk = sem("tk")
        tk_seen = sem("tk_seen")
        sm_step = sem("sm_step")
        sm_exp = sem("sm_exp")
        rt_done = sem("rt_done")
        rt_ready = sem("rt_ready")
        oh_ready = sem("oh_ready")
        oh_step = sem("oh_step")
        g_copied = sem("g_copied")
        NT = TB * PH
        G_PER = 16
        ROUNDS = GT // G_PER
        ES = 2 * NT
        EG = ES + 2
        EG_END = EG + T // G_PER
        ES_END = EG_END + ROUNDS
        GE = EB // ROUNDS
        assert ES_END <= EB - 2 and T % (2 * GT) == 0 and ROUNDS == 4

        up_v = expert_up[0].rearrange("(b p) (h d) -> h b p d", p=P, h=2)
        up_landed = [sem(f"up_landed{s}") for s in range(2)]
        ag_landed = [sem(f"ag_landed{s}") for s in range(2)]
        up_hi_done = sem("up_hi_done")
        up_ready = sem("up_ready")
        ag_full = sem("ag_full")
        ag_hi_done = sem("ag_hi_done")
        ag_ready = sem("ag_ready")
        f_done = sem("f_done")
        x1f_landed = sem("x1f_landed")
        half_read = sem("half_read")
        otr_done = sem("otr_done")
        o_copied = sem("o_copied")
        out_stored = sem("out_stored")

        def up_load(sp, h, i, s, first=False):
            n = h * EB + i
            if not first:
                sp.wait_ge(up_ready, n - 1)
                sp.wait_ge(ag_full, n - 1)
            sp.dma_start(up_raw[s][:, :], up_v[h, bass.ds(i, 1)].rearrange("a p d -> p (a d)"))\
              .then_inc(up_landed[s], 16)
            sp.dma_start(a_in[s][:, :], act_dram[bass.ds(i, 1)].rearrange("a p t -> p (a t)"))\
              .then_inc(ag_landed[s], 16)
            sp.dma_start(g_in[s][:, :], gate_dram[bass.ds(i, 1)].rearrange("a p t -> p (a t)"))\
              .then_inc(ag_landed[s], 16)

        def up_highs(act, h, i, s, m, first=False):
            n = h * EB + i
            act.wait_ge(up_landed[s], 16 * (h * (EB // 2) + m + 1))
            if not first:
                act.wait_ge(f_done, n - 1)
            act.activation(up_hi[s][:, :], up_raw[s][:, :], ACT.Copy).then_inc(up_hi_done, 1)
            act.wait_ge(ag_full, n + 1)
            act.activation(ag_hi[s][:, :], ag[s][:, :], ACT.Copy).then_inc(ag_hi_done, 1)

        def up_lows(dve, h, i, s, m, first=False):
            n = h * EB + i
            if not first:
                dve.wait_ge(f_done, n - 1)
            dve.wait_ge(ag_landed[s], 32 * (h * (EB // 2) + m + 1))
            if not first:
                dve.wait_ge(ag_ready, n - 1)
            dve.tensor_tensor(ag[s][:, :], a_in[s][:, :], g_in[s][:, :], ALU.mult).then_inc(ag_full, 1)
            dve.wait_ge(up_hi_done, n + 1)
            dve.tensor_tensor(up_lo[s][:, :], up_raw[s][:, :], up_hi[s][:, :].bitcast(F32),
                              ALU.subtract).then_inc(up_ready, 1)
            dve.wait_ge(ag_hi_done, n + 1)
            dve.tensor_tensor(ag_lo[s][:, :], ag[s][:, :], ag_hi[s][:, :].bitcast(F32),
                              ALU.subtract).then_inc(ag_ready, 1)

        with nc.Block() as block:
            @block.sync
            def _(sp):
                def step(i, s, last=False):
                    if not last:
                        sp.wait_ge(dtr_done, 4 * i + 4)
                        sp.dma_start(raw[s][:, :, :],
                                     down_v[bass.ds(i + 2, 1)].rearrange("a p (c d) -> p (a c) d", c=C))\
                          .then_inc(down_landed[s], 16)
                    sp.wait_ge(a_ready, i + 1)
                    sp.dma_start(act_dram[bass.ds(i, 1)].rearrange("a p t -> p (a t)"), aout[s][:, :])\
                      .then_inc(a_stored[s], 16)

                with sp.Fori(0, EG // 2 + 1) as m:
                    step(2 * m, 0)
                    step(2 * m + 1, 1)
                step(EG + 2, 0)
                with sp.Fori(0, T // GT // 2) as b:
                    for gs in range(2):
                        for k in range(ROUNDS):
                            step(EG + ROUNDS * (2 * b + gs) + 3 + k, (3 + k) % 2)
                            sp.wait_ge(g_copied, (2 * b + gs + 1) * (GT // 4))
                            eb = slice(k * GE, (k + 1) * GE)
                            sp.dma_start(gate_dram[eb, :, bass.ds((2 * b + gs) * GT, GT)]
                                         .rearrange("i j t -> j i t"),
                                         gbuf[gs][:, eb, :]).then_inc(g_stored[gs], 16)
                step(ES_END - 1, 1)
                with sp.Fori(ES_END // 2, EB // 2 - 1) as m:
                    step(2 * m, 0)
                    step(2 * m + 1, 1)
                for gs in range(2):
                    sp.wait_ge(g_stored[gs], 16 * ROUNDS * (T // GT // 2))
                sp.dma_start(x1f[:, :, :], x1_dram.rearrange("c p t -> p c t")).then_inc(x1f_landed, 16)
                for s in range(2):
                    sp.wait_ge(a_stored[s], 16)
                sp.wait_ge(dtr_done, 4 * (EB - 1))
                for s in range(2):
                    up_load(sp, 0, s, s, first=True)
                step(EB - 2, 0, last=True)
                step(EB - 1, 1, last=True)

            @block.tensor
            def _(pe):
                def quarter_in(i, s, q):
                    for r in range(4):
                        mm = pe.transpose(bank[q][:, r * P:(r + 1) * P], raw[s][:, 4 * q + r, :], ident[:, :])
                    mm.then_inc(dtr_done, 1)

                def block_products(i, s, m, extra=None, following=True):
                    if following:
                        pe.wait_ge(down_landed[1 - s], 16 * (m + s) + 16)
                    for q in range(4):
                        pe.wait_ge(d_lo, 4 * i + q + 1)
                        if following:
                            quarter_in(i + 1, 1 - s, q)
                        if q == 0 and not (isinstance(i, int) and i < 2):
                            pe.wait_ge(a_ready, i - 1)
                        for r in range(4):
                            cc = 4 * q + r
                            mm = three_pass(pe, bank[4 + s][:, :], s, cc, act_hi[:, cc, :], act_lo[:, cc, :],
                                            cc == 0, cc == C - 1)
                        if q == 3:
                            mm.then_inc(a_done, 1)
                        if extra:
                            extra(q)

                def pair(m):
                    for s in range(2):
                        block_products(2 * m + s, s, m)

                pe.wait_ge(down_landed[0], 16)
                for q in range(4):
                    quarter_in(0, 0, q)
                pair(0)
                with pe.Fori(1, ES // 2) as m:
                    pair(m)
                block_products(ES, 0, ES // 2)
                pe.wait_ge(sm_step, 4)
                for k, src in enumerate((top_all, i_all, j_all)):
                    if k == 2:
                        pe.wait_ge(rt_ready, 1)
                    for tb in range(TB):
                        mm = pe.transpose(bank[6 + k % 2][:, tb * P:(tb + 1) * P], src[:, tb, :], ident[:, :])
                    mm.then_inc(rt_done, 1)
                block_products(ES + 1, 1, ES // 2)

                def gates(n, q):
                    pe.wait_ge(oh_ready, n + 1)
                    if not (isinstance(n, int) and n < 2):
                        pe.wait_ge(g_copied, n - 1)
                    for t in range(4):
                        mm = pe.matmul(bank[6 + q % 2][:, t * P:(t + 1) * P], oh_j[q % 2][:, t, :],
                                       oh_g[q % 2][:, t, :], start=True, stop=True)
                    mm.then_inc(g_done, 1)

                def pair_with_gates(m):
                    for s in range(2):
                        w = 2 * m + s
                        block_products(EG + w, s, EG // 2 + m, extra=lambda q: gates(4 * w + q, q))

                pair_with_gates(0)
                with pe.Fori(1, (EG_END - EG) // 2) as m:
                    pair_with_gates(m)
                with pe.Fori(EG_END // 2, EB // 2 - 1) as m:
                    pair(m)
                block_products(EB - 2, 0, EB // 2 - 1)
                block_products(EB - 1, 1, EB // 2 - 1, following=False)

            @block.scalar
            def _(act):
                def high(i, s, q):
                    act.wait_ge(dtr_done, 4 * i + q + 1)
                    act.activation(w_hi_t[s][:, 4 * q:4 * q + 4, :],
                                   bank[q][:, :].rearrange("p (r e) -> p r e", r=4), ACT.Copy)\
                       .then_inc(d_hi, 1)

                def gelu(i, s, m):
                    act.wait_ge(a_done, i + 1)
                    if not (isinstance(m, int) and m == 0):
                        act.wait_ge(a_stored[s], 16 * m)
                    act.activation(aout[s][:, :], bank[4 + s][:, :], ACT.Gelu).then_inc(a_ready, 1)

                def pair(m):
                    for s in range(2):
                        for q in range(4):
                            high(2 * m + s + 1, 1 - s, q)
                        gelu(2 * m + s, s, m)

                for q in range(4):
                    high(0, 0, q)
                pair(0)
                with act.Fori(1, ES // 2) as m:
                    pair(m)
                act.wait_ge(sm_step, 1)
                act.activation(top_all[:, :, :], top_all[:, :, :], ACT.Exp).then_inc(sm_exp, 1)
                for q in range(4):
                    high(ES + 1, 1, q)
                gelu(ES, 0, ES // 2)
                for k, dst in enumerate((gate_t, i_t, j_t)):
                    act.wait_ge(rt_done, k + 1)
                    act.activation(dst[:, :], bank[6 + k % 2][:, :], ACT.Copy).then_inc(rt_ready, 1)
                for q in range(4):
                    high(ES + 2, 0, q)
                gelu(ES + 1, 1, ES // 2)

                def two_stored_blocks(b, first=False):
                    for gs in range(2):
                        if not first:
                            act.wait_ge(g_stored[gs], 16 * ROUNDS * b)
                        for j in range(ROUNDS):
                            s = j % 2
                            w = gs * ROUNDS + j
                            i = EG + 2 * ROUNDS * b + w
                            n = 4 * (2 * ROUNDS * b + w)
                            for q in range(4):
                                high(i + 1, 1 - s, q)
                                act.wait_ge(g_done, n + q + 1)
                                off = j * G_PER + 4 * q
                                act.activation(gbuf[gs][:, :, off:off + 4].rearrange("p i t -> p t i"),
                                               bank[6 + q % 2][:, :].rearrange("p (t i) -> p t i", t=4),
                                               ACT.Copy).then_inc(g_copied, 1)
                            gelu(i, s, EG // 2 + ROUNDS * b + w // 2)

                two_stored_blocks(0, first=True)
                with act.Fori(1, T // GT // 2) as b:
                    two_stored_blocks(b)
                with act.Fori(EG_END // 2, EB // 2 - 1) as m:
                    pair(m)
                for q in range(4):
                    high(EB - 1, 1, q)
                gelu(EB - 2, 0, EB // 2 - 1)
                act.wait_ge(dtr_done, 4 * EB)
                for s in range(2):
                    up_highs(act, 0, s, s, 0, first=True)
                gelu(EB - 1, 1, EB // 2 - 1)

            @block.vector
            def _(dve):
                def low(i, s, q):
                    dve.wait_ge(d_hi, 4 * i + q + 1)
                    dve.tensor_tensor(w_lo_t[s][:, 4 * q:4 * q + 4, :],
                                      bank[q][:, :].rearrange("p (r e) -> p r e", r=4),
                                      w_hi_t[s][:, 4 * q:4 * q + 4, :].bitcast(F32), ALU.subtract)\
                       .then_inc(d_lo, 1)

                STEPS = 19
                BEFORE_MAX = (1, 2, 3, 4, 5, 6, 7, 8, 10, 11, 12, 13)

                def step(v, k, ins):
                    ins.then_inc(tk, 1)
                    dve.wait_ge(tk, STEPS * v + k)
                    if k in BEFORE_MAX:
                        dve.sem_inc(tk_seen, 1)

                def top_keys(v, tb, h2, p):
                    k = 1 + 4 * p
                    if p == 0:
                        step(v, 1, dve.tensor_scalar(srow[:, :, :], s_all[:, tb, bass.ds(h2, 2), :], 1.0, None,
                                                     ALU.mult))
                    step(v, k + 1, dve.max(val[:, p, 0:8], srow[:, p, :]))
                    dve.max_index(idx[:, p, 0:8], val[:, p, 0:8], srow[:, p, :])
                    step(v, k + 2, dve.match_replace(srow2[:, p, :], val[:, p, 0:8], srow[:, p, :], NEG))
                    step(v, k + 3, dve.max(val[:, p, 8:16], srow2[:, p, :]))
                    step(v, k + 4, dve.max_index(idx[:, p, 8:16], val[:, p, 8:16], srow2[:, p, :]))

                def top_sums(v):
                    step(v, 10, dve.tensor_tensor(
                        cand[:, :, :], val[:, 0, :].unsqueeze(2).to_broadcast([P, TOPK, TOPK]),
                        val[:, 1, :].unsqueeze(1).to_broadcast([P, TOPK, TOPK]), ALU.add))
                    flat, flat2 = (t[:, :, :].rearrange("p a b -> p (a b)") for t in (cand, cand2))
                    step(v, 11, dve.max(topv[:, 0:8], flat))
                    dve.max_index(pos[:, 0:8], topv[:, 0:8], flat)
                    step(v, 12, dve.match_replace(flat2, topv[:, 0:8], flat, NEG))
                    step(v, 13, dve.max(topv[:, 8:16], flat2))
                    step(v, 14, dve.max_index(pos[:, 8:16], topv[:, 8:16], flat2))

                def indices(v, tb, h2):
                    dve.tensor_scalar(posab[:, 0, :], pos[:, :], 4, None, ALU.logical_shift_right)
                    step(v, 15, dve.tensor_scalar(posab[:, 1, :], pos[:, :], TOPK - 1, None, ALU.bitwise_and))
                    dve.tensor_copy(posf[:, :, :], posab[:, :, :])
                    step(v, 16, dve.tensor_copy(idxf[:, :, :], idx[:, :, :]))
                    step(v, 17, dve.tensor_tensor(
                        pick[:, :, :, :].rearrange("p a k m -> p (a k) m"),
                        posf[:, :, :].rearrange("p a k -> p (a k)").unsqueeze(2).to_broadcast([P, 2 * TOPK, TOPK]),
                        iota_keys[:, 0:TOPK].unsqueeze(1).to_broadcast([P, 2 * TOPK, TOPK]), ALU.is_equal))
                    step(v, 18, dve.tensor_tensor(
                        pick2[:, :, :, :], pick[:, :, :, :],
                        idxf[:, :, :].unsqueeze(2).to_broadcast([P, 2, TOPK, TOPK]), ALU.mult))
                    hk = bass.ds(h2 * (TOPK // 2), TOPK)
                    dve.tensor_reduce(i_all[:, tb, hk], pick2[:, 0, :, :], AX.X, ALU.add)
                    dve.tensor_reduce(j_all[:, tb, hk], pick2[:, 1, :, :], AX.X, ALU.add)
                    step(v, 19, dve.tensor_scalar(top_all[:, tb, hk], topv[:, :], topv[:, 0:1], None,
                                                  ALU.subtract))

                for q in range(4):
                    low(0, 0, q)
                for tb in range(TB):
                    with dve.Fori(0, PH) as m:
                        v = tb * PH + m
                        h2 = 2 * m
                        low(2 * v + 1, 1, 0)
                        top_keys(v, tb, h2, 0)
                        low(2 * v + 1, 1, 1)
                        low(2 * v + 1, 1, 2)
                        top_keys(v, tb, h2, 1)
                        low(2 * v + 1, 1, 3)
                        low(2 * v + 2, 0, 0)
                        top_sums(v)
                        low(2 * v + 2, 0, 1)
                        low(2 * v + 2, 0, 2)
                        indices(v, tb, h2)
                        low(2 * v + 2, 0, 3)
                dve.sem_inc(sm_step, 1)
                dve.wait_ge(sm_exp, 1)
                heads = top_all[:, :, :].rearrange("p b (h k) -> p (b h) k", k=TOPK)
                dve.tensor_reduce(zsum[:, :], heads, AX.X, ALU.add).then_inc(sm_step, 1)
                dve.wait_ge(sm_step, 2)
                low(ES + 1, 1, 0)
                dve.reciprocal(zsum[:, :], zsum[:, :]).then_inc(sm_step, 1)
                dve.wait_ge(sm_step, 3)
                low(ES + 1, 1, 1)
                dve.tensor_tensor(heads, heads, zsum[:, :].unsqueeze(2).to_broadcast([P, TB * PH, TOPK]),
                                  ALU.mult).then_inc(sm_step, 1)
                low(ES + 1, 1, 2)
                low(ES + 1, 1, 3)
                for q in range(4):
                    low(ES + 2, 0, q)
                dve.wait_ge(rt_ready, 3)

                def one_hots(n, s):
                    t = bass.ds(4 * n, 4)
                    if not (isinstance(n, int) and n < 2):
                        dve.wait_ge(g_done, n - 1)
                    keys = iota_keys[:, :].unsqueeze(1).to_broadcast([P, 4, P])
                    dve.tensor_tensor(oh_i[s][:, :, :], i_t[:, t].unsqueeze(2).to_broadcast([P, 4, P]), keys,
                                      ALU.is_equal).then_inc(oh_step, 1)
                    dve.tensor_tensor(oh_j[s][:, :, :], j_t[:, t].unsqueeze(2).to_broadcast([P, 4, P]), keys,
                                      ALU.is_equal)
                    dve.wait_ge(oh_step, n + 1)
                    dve.tensor_tensor(oh_g[s][:, :, :], oh_i[s][:, :, :],
                                      gate_t[:, t].unsqueeze(2).to_broadcast([P, 4, P]), ALU.mult)\
                       .then_inc(oh_ready, 1)

                def pair_with_gates(m):
                    for s in range(2):
                        for q in range(4):
                            one_hots(4 * (2 * m + s) + q, q % 2)
                            low(EG + 2 * m + s + 1, 1 - s, q)

                pair_with_gates(0)
                with dve.Fori(1, (EG_END - EG) // 2) as m:
                    pair_with_gates(m)
                with dve.Fori(EG_END // 2, EB // 2 - 1) as m:
                    for s in range(2):
                        for q in range(4):
                            low(2 * m + s + 1, 1 - s, q)
                for q in range(4):
                    low(EB - 1, 1, q)
                dve.wait_ge(a_done, EB - 1)
                for s in range(2):
                    up_lows(dve, 0, s, s, 0, first=True)

        with nc.Block() as block:
            @block.sync
            def _(sp):
                for s in range(2):
                    sp.wait_ge(a_stored[s], 16 * (EB // 2))
                for h in range(2):
                    with sp.Fori(1 if h == 0 else 0, EB // 2) as m:
                        for s in range(2):
                            up_load(sp, h, 2 * m + s, s)
                for tb in range(TB):
                    sp.wait_ge(o_copied, 4 * (tb + 1))
                    sp.dma_start(out_v[tb * P:(tb + 1) * P, :], orow[tb][:, :]).then_inc(out_stored, 16)
                sp.wait_ge(out_stored, 16 * TB)

            @block.tensor
            def _(pe):
                def experts(h, i, s, start, stop):
                    n = h * EB + i
                    pe.wait_ge(up_ready, n + 1)
                    pe.wait_ge(ag_ready, n + 1)
                    for dc in range(HC):
                        cols = slice(dc * P, (dc + 1) * P)
                        pe.matmul(bank[dc][:, :], up_hi[s][:, cols], ag_hi[s][:, :], start=start, stop=False,
                                  skip_group_check=True)
                        pe.matmul(bank[dc][:, :], up_hi[s][:, cols], ag_lo[s][:, :], start=False, stop=False,
                                  skip_group_check=True)
                        mm = pe.matmul(bank[dc][:, :], up_lo[s][:, cols], ag_hi[s][:, :], start=False,
                                       stop=stop, skip_group_check=True)
                    mm.then_inc(f_done, 1)

                for h in range(2):
                    if h:
                        pe.wait_ge(half_read, HC)
                    experts(h, 0, 0, True, False)
                    experts(h, 1, 1, False, False)
                    with pe.Fori(1, EB // 2 - 1) as m:
                        experts(h, 2 * m, 0, False, False)
                        experts(h, 2 * m + 1, 1, False, False)
                    experts(h, EB - 2, 0, False, False)
                    experts(h, EB - 1, 1, False, True)
                pe.wait_ge(half_read, 2 * HC)
                for tb in range(TB):
                    for q in range(4):
                        n = 4 * tb + q
                        if n >= 8:
                            pe.wait_ge(o_copied, n - 7)
                        for r in range(4):
                            mm = pe.transpose(bank[n % 8][:, r * P:(r + 1) * P],
                                              x1f[:, 4 * q + r, tb * P:(tb + 1) * P], ident[:, :])
                        mm.then_inc(otr_done, 1)

            @block.scalar
            def _(act):
                for h in range(2):
                    with act.Fori(1 if h == 0 else 0, EB // 2) as m:
                        up_highs(act, h, 2 * m, 0, m)
                        up_highs(act, h, 2 * m + 1, 1, m)

            @block.vector
            def _(dve):
                for h in range(2):
                    with dve.Fori(1 if h == 0 else 0, EB // 2) as m:
                        up_lows(dve, h, 2 * m, 0, m)
                        up_lows(dve, h, 2 * m + 1, 1, m)
                    if h == 0:
                        dve.wait_ge(x1f_landed, 16)
                    dve.wait_ge(f_done, (h + 1) * EB)
                    for dc in range(HC):
                        n = h * HC + dc
                        dve.scalar_tensor_tensor(out=x1f[:, n, :], in0=bank[dc][:, :],
                                                 scalar=mod[:, 5 * C + n:5 * C + n + 1], in1=x1f[:, n, :],
                                                 op0=ALU.mult, op1=ALU.add).then_inc(half_read, 1)
                for tb in range(TB):
                    for q in range(4):
                        n = 4 * tb + q
                        dve.wait_ge(otr_done, n + 1)
                        dve.tensor_copy(orow[tb][:, 4 * q * P:(4 * q + 4) * P], bank[n % 8][:, :])\
                           .then_inc(o_copied, 1)


_INS = ['x', 'c', 'w_ada', 'b_ada', 'norm1_g', 'w_in', 'q_norm_g', 'k_norm_g', 'attn_sinks', 'pool_group_w',
        'pool_scale', 'w_branch_attn', 'w_branch_pool', 'w_out', 'norm2_g', 'w_query', 'sub_keys',
        'expert_down', 'expert_up']


def kernel(**inputs):
    import numpy as _np
    import concourse.bacc as _bacc
    from concourse import mybir as _mybir
    from concourse.bass_utils import run_bass_kernel_spmd as _run

    nc = _bacc.Bacc("TRN2", target_bir_lowering=False, num_devices=1)
    arrays, args = {}, []
    for name in _INS:
        a = _np.ascontiguousarray(inputs[name])
        arrays[f"in_{name}"] = a
        args.append(nc.dram_tensor(f"in_{name}", a.shape, _mybir.dt.from_np(a.dtype), kind="ExternalInput").ap())
    args.append(nc.dram_tensor("out_x", inputs["x"].shape, _mybir.dt.float32, kind="ExternalOutput").ap())
    build(nc, *args)
    r = _run(nc, [arrays], core_ids=[0])
    return r.results[0]["out_x"]
```
